# Optimizing a Trainium2 kernel written in Bass

```python
import jax, jax.numpy as jnp
from jax import lax
import numpy as np

D_MODEL = 1024
BATCH = 1
SEQ = 512
DEPTH = 1

GDN_HEADS = 8
GDN_HEAD_DIM = 128
GDN_WIDTH = GDN_HEADS * GDN_HEAD_DIM
CONV_WIDTH = 4
GDN_CHUNK = 64
FOX_HEADS = 16
FOX_HEAD_DIM = 64
FOX_WIDTH = FOX_HEADS * FOX_HEAD_DIM
FOX_BLOCK = 128
D_FF = -(-8 * D_MODEL // (3 * 256)) * 256
EPS = 1e-6

IN_SPLITS = (
    GDN_WIDTH, GDN_WIDTH, GDN_WIDTH,
    GDN_WIDTH,
    GDN_HEADS, GDN_HEADS,
    FOX_WIDTH, FOX_WIDTH, FOX_WIDTH,
    FOX_HEADS,
    FOX_WIDTH,
    D_MODEL, D_MODEL,
)
D_IN = sum(IN_SPLITS)

kernel_name = "hybrid_gdn_fox_gated_merge"

def rms_norm(x, w):
    xf = x.astype(jnp.float32)
    y = xf * lax.rsqrt(jnp.mean(xf * xf, axis=-1, keepdims=True) + EPS)
    return (y * w.astype(jnp.float32)).astype(x.dtype)

def l2_normalize(x):
    xf = x.astype(jnp.float32)
    return xf * lax.rsqrt(jnp.sum(xf * xf, axis=-1, keepdims=True) + EPS)

def causal_depthwise_conv(x, w):
    c = x.shape[-1]
    return lax.conv_general_dilated(
        x, w[:, None, :].astype(x.dtype), window_strides=(1,),
        padding=[(CONV_WIDTH - 1, 0)],
        dimension_numbers=("NWC", "WIO", "NWC"), feature_group_count=c)

def gated_delta_rule_chunked(q, k, v, g, beta):
    b, s, h, dk = q.shape
    dv = v.shape[-1]
    n = s // GDN_CHUNK
    c = GDN_CHUNK

    def chunks(t):
        return t.astype(jnp.float32).reshape(b, n, c, h, -1).transpose(0, 3, 1, 2, 4)

    q = chunks(q) * (dk ** -0.5)
    k = chunks(k)
    v = chunks(v)
    g = g.astype(jnp.float32).reshape(b, n, c, h).transpose(0, 3, 1, 2)
    beta = beta.astype(jnp.float32).reshape(b, n, c, h).transpose(0, 3, 1, 2)
    gc = jnp.cumsum(g, axis=-1)

    tri = jnp.tril(jnp.ones((c, c), dtype=bool))
    strict = jnp.tril(jnp.ones((c, c), dtype=bool), -1)
    diff = gc[..., :, None] - gc[..., None, :]
    decay = jnp.where(tri, jnp.exp(jnp.where(tri, diff, 0.0)), 0.0)

    kb = k * beta[..., None]
    vb = v * beta[..., None]
    lower = jnp.where(strict, jnp.einsum('bhncd,bhnsd->bhncs', kb, k) * decay, 0.0)
    a_mat = lower + jnp.eye(c, dtype=jnp.float32)
    rhs = jnp.concatenate([vb, kb * jnp.exp(gc)[..., None]], axis=-1)
    sol = lax.linalg.triangular_solve(a_mat, rhs, left_side=True, lower=True,
                                      unit_diagonal=True)
    u = sol[..., :dv]
    w = sol[..., dv:]
    qk = jnp.where(tri, jnp.einsum('bhncd,bhnsd->bhncs', q, k) * decay, 0.0)

    def step(state, inp):
        q_n, k_n, u_n, w_n, qk_n, gc_n = inp
        v_new = u_n - jnp.einsum('bhcd,bhde->bhce', w_n, state)
        o = (jnp.einsum('bhcd,bhde->bhce', q_n * jnp.exp(gc_n)[..., None], state)
             + jnp.einsum('bhcs,bhse->bhce', qk_n, v_new))
        g_last = gc_n[..., -1]
        k_dec = k_n * jnp.exp(g_last[..., None] - gc_n)[..., None]
        state = (state * jnp.exp(g_last)[..., None, None]
                 + jnp.einsum('bhcd,bhce->bhde', k_dec, v_new))
        return state, o

    xs = tuple(jnp.moveaxis(t, 2, 0) for t in (q, k, u, w, qk, gc))
    state0 = jnp.zeros((b, h, dk, dv), jnp.float32)
    _, o = lax.scan(step, state0, xs)
    o = jnp.moveaxis(o, 0, 2)
    return o.transpose(0, 2, 3, 1, 4).reshape(b, s, h, dv)

def forgetting_attention(q, k, v, log_f):
    b, s, h, d = q.shape
    nb = s // FOX_BLOCK
    scale = d ** -0.5
    cum = jnp.cumsum(log_f.astype(jnp.float32), axis=1)
    cum_k = cum.transpose(0, 2, 1)
    q_blocks = q.reshape(b, nb, FOX_BLOCK, h, d).transpose(1, 0, 2, 3, 4)
    c_blocks = cum.reshape(b, nb, FOX_BLOCK, h).transpose(1, 0, 3, 2)
    kpos = jnp.arange(s)

    def one_block(args):
        q_i, c_i, i = args
        sc = jnp.einsum('bqhd,bkhd->bhqk', q_i, k).astype(jnp.float32) * scale
        sc = sc + c_i[..., :, None] - cum_k[:, :, None, :]
        qpos = i * FOX_BLOCK + jnp.arange(FOX_BLOCK)
        mask = kpos[None, :] <= qpos[:, None]
        sc = jnp.where(mask, sc, -jnp.inf)
        p = jax.nn.softmax(sc, axis=-1).astype(v.dtype)
        return jnp.einsum('bhqk,bkhd->bqhd', p, v)

    out = lax.map(one_block, (q_blocks, c_blocks, jnp.arange(nb)))
    return out.transpose(1, 0, 2, 3, 4).reshape(b, s, h, d)

def hybrid_mixer(h, w_in, conv_w, a_log, dt_bias, gdn_norm_w, fox_f_bias,
                 w_branch_a, w_branch_b, w_out):
    b, s, _ = h.shape
    proj = h @ w_in
    offs = np.cumsum(np.array(IN_SPLITS))[:-1].tolist()
    (gq, gk, gv, gz, ga, gb, fq, fk, fv, ff, fo, mga, mgb) = jnp.split(proj, offs, axis=-1)

    qkv = jax.nn.silu(causal_depthwise_conv(jnp.concatenate([gq, gk, gv], axis=-1), conv_w))
    cq, ck, cv = jnp.split(qkv, 3, axis=-1)
    cq = l2_normalize(cq.reshape(b, s, GDN_HEADS, GDN_HEAD_DIM))
    ck = l2_normalize(ck.reshape(b, s, GDN_HEADS, GDN_HEAD_DIM))
    cv = cv.reshape(b, s, GDN_HEADS, GDN_HEAD_DIM)
    g = -jnp.exp(a_log.astype(jnp.float32)) * jax.nn.softplus(
        ga.astype(jnp.float32) + dt_bias.astype(jnp.float32))
    beta = jax.nn.sigmoid(gb.astype(jnp.float32))
    o_a = gated_delta_rule_chunked(cq, ck, cv, g, beta)
    o_a = o_a * lax.rsqrt(jnp.mean(o_a * o_a, axis=-1, keepdims=True) + EPS)
    o_a = o_a * gdn_norm_w.astype(jnp.float32) * jax.nn.silu(
        gz.astype(jnp.float32).reshape(b, s, GDN_HEADS, GDN_HEAD_DIM))
    o_a = o_a.reshape(b, s, GDN_WIDTH).astype(h.dtype)

    log_f = jax.nn.log_sigmoid(ff.astype(jnp.float32) + fox_f_bias.astype(jnp.float32))
    o_b = forgetting_attention(fq.reshape(b, s, FOX_HEADS, FOX_HEAD_DIM),
                               fk.reshape(b, s, FOX_HEADS, FOX_HEAD_DIM),
                               fv.reshape(b, s, FOX_HEADS, FOX_HEAD_DIM), log_f)
    o_b = o_b.reshape(b, s, FOX_WIDTH) * jax.nn.sigmoid(fo)

    y = (jax.nn.sigmoid(mga) * (o_a @ w_branch_a)
         + jax.nn.sigmoid(mgb) * (o_b @ w_branch_b))
    return y @ w_out

def swiglu(h, w_gate, w_up, w_down):
    return (jax.nn.silu(h @ w_gate) * (h @ w_up)) @ w_down

def setup_inputs(seed: int = 0) -> dict:
    key = jax.random.key(seed)
    ks = jax.random.split(key, 20)
    f32 = jnp.float32

    def dense(k, fan_in, fan_out):
        return jax.random.normal(k, (DEPTH, fan_in, fan_out), f32) * fan_in ** -0.5

    def gain(k, n):
        return 1.0 + 0.02 * jax.random.normal(k, (DEPTH, n), f32)

    x = jax.random.normal(ks[0], (BATCH, SEQ, D_MODEL), f32)
    dt = jnp.exp(jax.random.uniform(ks[5], (DEPTH, GDN_HEADS), f32,
                                    minval=np.log(1e-3), maxval=np.log(1e-1)))
    return {
        "x": x,
        "norm_mix_w": gain(ks[1], D_MODEL),
        "w_in": dense(ks[2], D_MODEL, D_IN),
        "conv_w": jax.random.normal(ks[3], (DEPTH, CONV_WIDTH, 3 * GDN_WIDTH), f32) * CONV_WIDTH ** -0.5,
        "a_log": jnp.log(jax.random.uniform(ks[4], (DEPTH, GDN_HEADS), f32, minval=1.0, maxval=16.0)),
        "dt_bias": dt + jnp.log(-jnp.expm1(-dt)),
        "gdn_norm_w": gain(ks[6], GDN_HEAD_DIM),
        "fox_f_bias": jax.random.uniform(ks[7], (DEPTH, FOX_HEADS), f32, minval=1.0, maxval=4.0),
        "w_branch_a": dense(ks[8], GDN_WIDTH, D_MODEL),
        "w_branch_b": dense(ks[9], FOX_WIDTH, D_MODEL),
        "w_out": dense(ks[10], D_MODEL, D_MODEL),
        "norm_ffn_w": gain(ks[11], D_MODEL),
        "w_gate": dense(ks[12], D_MODEL, D_FF),
        "w_up": dense(ks[13], D_MODEL, D_FF),
        "w_down": dense(ks[14], D_FF, D_MODEL),
        "norm_final_w": 1.0 + 0.02 * jax.random.normal(ks[15], (D_MODEL,), f32),
    }

def reference(x, norm_mix_w, w_in, conv_w, a_log, dt_bias, gdn_norm_w, fox_f_bias,
              w_branch_a, w_branch_b, w_out, norm_ffn_w, w_gate, w_up, w_down,
              norm_final_w):
    h = x
    for l in range(DEPTH):
        h = h + hybrid_mixer(rms_norm(h, norm_mix_w[l]), w_in[l], conv_w[l], a_log[l],
                             dt_bias[l], gdn_norm_w[l], fox_f_bias[l],
                             w_branch_a[l], w_branch_b[l], w_out[l])
        h = h + swiglu(rms_norm(h, norm_ffn_w[l]), w_gate[l], w_up[l], w_down[l])
    return rms_norm(h, norm_final_w)


_drawn_inputs = setup_inputs


def setup_inputs(seed=0):
    import zlib

    import numpy as np

    out = dict(_drawn_inputs(seed))
    spreads = {}
    factors = {'norm_mix_w': 4.354, 'gdn_norm_w': 8.0, 'norm_ffn_w': 13.378, 'norm_final_w': 8.189}
    for name, (base, spread) in spreads.items():
        noise = np.random.default_rng([zlib.crc32(name.encode()), seed]).standard_normal(out[name].shape)
        drawn = base * np.exp(spread * noise) if base else spread * noise
        out[name] = __import__('jax').numpy.asarray(drawn.astype(out[name].dtype))
    for name, factor in factors.items():
        out[name] = (out[name] * factor).astype(out[name].dtype)
    return out
```

```python
from contextlib import ExitStack

import concourse.bass as bass
from concourse import mybir

ALU = mybir.AluOpType
ACT = mybir.ActivationFunctionType
F32 = mybir.dt.float32
F32R = mybir.dt.float32r
BF16 = mybir.dt.bfloat16

P = 128
EPS = 1e-6
NEG = -1e30


def hybrid_block(nc, x, norm_mix_w, w_in, conv_w, a_log, dt_bias, gdn_norm_w, fox_f_bias, w_branch_a,
                 w_branch_b, w_out, norm_ffn_w, w_gate, w_up, w_down, norm_final_w, out):
    _, T, D = x.shape
    DK = gdn_norm_w.shape[1]
    H = a_log.shape[1]
    FH = fox_f_bias.shape[1]
    FD = D // FH
    TAPS = conv_w.shape[1]
    F = w_gate.shape[2]
    C = P
    TT, KT, FT = T // P, D // P, F // P
    NCONV = 3 * H
    assert (T, KT, DK, H, FH, FD, TAPS) == (512, 8, P, 8, 16, 64, 4) and FT % 2 == 0
    W = H * DK
    GZ, GA = 3 * W, 4 * W
    FQ = GA + 2 * H
    FK, FV, FF = FQ + D, FQ + 2 * D, FQ + 3 * D
    FO = FF + FH
    MA, MB = FO + D, FO + 2 * D
    UNIT = KT * P

    QKV0 = 0
    Z0 = QKV0 + NCONV // 4
    A0 = Z0 + H // 4
    FOX0 = A0 + 2 * KT // 4
    B0 = FOX0 + FH // 2
    OUT0 = B0 + 2 * KT // 4
    FFN0 = OUT0 + KT // 4
    DOWN0 = FFN0 + 2 * FT // 4

    NMIX, NFFN, GNW = TAPS * NCONV, TAPS * NCONV + KT, TAPS * NCONV + 2 * KT
    NPRM = GNW + 1

    cum_dram = nc.dram_tensor("cum_dram", [FH, T], F32).ap()

    with ExitStack() as ctx:
        def sem(name):
            return ctx.enter_context(nc.semaphore(name))

        def keep(name, shape, dt=F32):
            return ctx.enter_context(nc.sbuf_tensor(name, shape, dt))

        h_hi = keep("h_hi", [P, KT, T], F32R)
        h_lo = keep("h_lo", [P, KT, T], F32R)
        raw = keep("raw", [P, 4, UNIT])
        w_hi = keep("w_hi", [P, 2, UNIT], F32R)
        w_lo = keep("w_lo", [P, 2, UNIT], F32R)
        mixT = keep("mixT", [P, KT, T])
        ident = keep("ident", [P, P])
        step = keep("step", [P, 7 * P])
        after = keep("after", [P, P])
        low = keep("low", [P, P])
        pair_neg = keep("pair_neg", [P, P])
        blk_neg = keep("blk_neg", [P, 5, P])
        ident_b = keep("ident_b", [P, P], BF16)
        mask_b = keep("mask_b", [P, P], BF16)
        half_neg = keep("half_neg", [P, 2 * H])
        prm = keep("prm", [P, NPRM])
        gate = keep("gate", [P, 2, T])
        tmp = keep("tmp", [P, 2, T])
        ss = keep("ss", [P, TT])
        ms = keep("ms", [P, TT])
        rstd = keep("rstd", [P, TT])

        with ExitStack() as part:
            def sb(name, shape, dt=F32):
                return part.enter_context(nc.sbuf_tensor(name, shape, dt))

            x_nat = sb("x_nat", [P, TT, D])
            xn = sb("xn", [P, TT, D])
            prm_rows = sb("prm_rows", [P, P])
            wsm = sb("wsm", [P, KT, 32])
            wsm_hi = sb("wsm_hi", [P, KT, 32], F32R)
            wsm_lo = sb("wsm_lo", [P, KT, 32], F32R)
        with ExitStack() as part:
            def sb(name, shape, dt=F32):
                return part.enter_context(nc.sbuf_tensor(name, shape, dt))

            qkv = sb("qkv", [P, NCONV, T])
            qS = sb("qS", [P, H, C])
            kS = sb("kS", [P, H, C])
            vS = sb("vS", [P, H, C])
            sq = sb("sq", [P, 2 * H, C])
            gm = sb("gm", [P, H, C])
            E = sb("E", [P, H, C])
            L = sb("L", [P, H, C])
            Yn = sb("Yn", [P, H, C])
            Kd = sb("Kd", [P, H, C])
            Vb = sb("Vb", [P, H, C])
            qk = sb("qk", [P, H, C])
            qkT = sb("qkT", [P, H, C])
            S = sb("S", [P, H, DK])
            gv = sb("gv", [P, TT, 3 * H])
            gabs = sb("gabs", [P, TT, 3 * H])
            sp = sb("sp", [P, TT, 3 * H])
            gb = sb("gb", [P, TT, H])
            beta = sb("beta", [P, TT * H])
            g = sb("g", [P, TT * H])
            gexp = sb("gexp", [P, 3, TT * H])
            bias_dt = sb("bias_dt", [P, H])
            bias_ff = sb("bias_ff", [P, FH])
            alog = sb("alog", [P, H])
            cum = sb("cum", [FH, T])
            nsum = sb("nsum", [P, 2 * H])
            rn = sb("rn", [P, 2 * H])
            bn = sb("bn", [P, H])
            bn2 = sb("bn2", [P, H])
            c1 = sb("c1", [P, H])
            oss = sb("oss", [P, H])
            osc = sb("osc", [P, H])
            cv = tmp
            Tm, Zm = sq[:, 0:H, :], sq[:, H:2 * H, :]
            Eb, X = gm, gm
            w = E
            o = vS
            of = qk
        with ExitStack() as part:
            def sb(name, shape, dt=F32):
                return part.enter_context(nc.sbuf_tensor(name, shape, dt))

            vT = sb("vT", [P, T])
            v_nat = sb("v_nat", [P, TT, P])
            qx = sb("qx", [FD, 2, T])
            kx = sb("kx", [FD, 2, T])
            NS = TT * (TT + 1) // 2 * P
            probs = sb("probs", [P, 2 * NS])
            probsT = sb("probsT", [P, 2 * NS])
            cumb = sb("cumb", [P, 2, T])
            scratch = sb("scratch", [P, 2 * TT])
            nmax = sb("nmax", [P, 2 * TT])
            psum_p = sb("psum_p", [P, 2 * TT])
            rsum = sb("rsum", [P, 2 * TT])
            o_nat = sb("o_nat", [P, TT, P])
            efo = sb("efo", [P, T])
            sfo = sb("sfo", [P, T])
            a_hi = sb("a_hi", [P, KT, T], F32R)
            a_lo = sb("a_lo", [P, KT, T], F32R)
            b_hi = sb("b_hi", [P, KT, T], F32R)
            b_lo = sb("b_lo", [P, KT, T], F32R)
        with ExitStack() as part:
            def sb(name, shape, dt=F32):
                return part.enter_context(nc.sbuf_tensor(name, shape, dt))

            x_res = sb("x_res", [P, TT, D])
            with ExitStack() as inner:
                xn2 = inner.enter_context(nc.sbuf_tensor("xn2", [P, TT, D], F32))
            f_hi = sb("f_hi", [P, FT, T], F32R)
            f_lo = sb("f_lo", [P, FT, T], F32R)
            wfin = sb("wfin", [P, D])
        back = tmp

        ps = ctx.enter_context(nc.psum_tensor("ps", [P, 8, 512], F32))

        x_loaded = sem("x_loaded")
        prm_loaded = sem("prm_loaded")
        small_loaded = sem("small_loaded")
        w_loaded = [sem(f"w_loaded{s}") for s in range(4)]
        w_high = sem("w_high")
        w_low = sem("w_low")
        unit_done = sem("unit_done")
        consts_ready = sem("consts_ready")
        prm_turned = sem("prm_turned")
        prm_ready = sem("prm_ready")
        sq_summed = sem("sq_summed")
        ms_ready = sem("ms_ready")
        rstd_ready = sem("rstd_ready")
        x_scaled = sem("x_scaled")
        x_turned = sem("x_turned")
        h_high = sem("h_high")
        h_low = sem("h_low")
        wsm_high = sem("wsm_high")
        wsm_ready = sem("wsm_ready")
        small_done = sem("small_done")
        small_taken = sem("small_taken")
        gate_exp = sem("gate_exp")
        gate_step = sem("gate_step")
        gate_sums = sem("gate_sums")
        gexp_ready = sem("gexp_ready")
        cum_taken = sem("cum_taken")
        cum_stored = sem("cum_stored")
        conv_seed = sem("conv_seed")
        conv_tap = sem("conv_tap")
        conv_bank = sem("conv_bank")
        conv_out = sem("conv_out")
        state_zero = sem("state_zero")
        staged = sem("staged")
        squared = sem("squared")
        sums_done = sem("sums_done")
        sums_taken = sem("sums_taken")
        rn_ready = sem("rn_ready")
        row_step = sem("row_step")
        gm_ready = sem("gm_ready")
        D_done = sem("D_done")
        E_exp = sem("E_exp")
        E_masked = sem("E_masked")
        Eb_ready = sem("Eb_ready")
        k_turned = sem("k_turned")
        v_turned = sem("v_turned")
        Kd_ready = sem("Kd_ready")
        Vb_ready = sem("Vb_ready")
        G_done = sem("G_done")
        qk_done = sem("qk_done")
        L_ready = sem("L_ready")
        qk_ready = sem("qk_ready")
        T_step = sem("T_step")
        Z_turned = sem("Z_turned")
        Z_ready = sem("Z_ready")
        qk_turned = sem("qk_turned")
        qkT_ready = sem("qkT_ready")
        Y_done = sem("Y_done")
        Y_ready = sem("Y_ready")
        ZT_done = sem("ZT_done")
        ZT_ready = sem("ZT_ready")
        ks_done = sem("ks_done")
        qs_done = sem("qs_done")
        X_ready = sem("X_ready")
        qs_ready = sem("qs_ready")
        w_done = sem("w_done")
        w_ready = sem("w_ready")
        qkw_done = sem("qkw_done")
        S_done = sem("S_done")
        o_ready = sem("o_ready")
        S_ready = sem("S_ready")
        o_squared = sem("o_squared")
        osc_step = sem("osc_step")
        osc_pow = sem("osc_pow")
        of_ready = sem("of_ready")
        of_turned = sem("of_turned")
        oT_ready = sem("oT_ready")
        z_gate = sem("z_gate")
        z_mul = sem("z_mul")
        a_high = sem("a_high")
        a_low = sem("a_low")
        ma_gate = sem("ma_gate")
        a_merged = sem("a_merged")
        v_taken = sem("v_taken")
        q_taken = sem("q_taken")
        k_taken = sem("k_taken")
        fo_exp = sem("fo_exp")
        fo_step = sem("fo_step")
        cumb_loaded = sem("cumb_loaded")
        score_done = sem("score_done")
        score_taken = sem("score_taken")
        probs_ready = sem("probs_ready")
        probs_turned = sem("probs_turned")
        probsT_ready = sem("probsT_ready")
        rsum_ready = sem("rsum_ready")
        pv_done = sem("pv_done")
        o_taken = sem("o_taken")
        o_turned = sem("o_turned")
        v_back = sem("v_back")
        v_ready = sem("v_ready")
        b_mul = sem("b_mul")
        b_high = sem("b_high")
        b_low = sem("b_low")
        mb_gate = sem("mb_gate")
        b_gated = sem("b_gated")
        y_sum = sem("y_sum")
        y_high = sem("y_high")
        y_low = sem("y_low")
        xres_loaded = sem("xres_loaded")
        out_taken = sem("out_taken")
        out_turned = sem("out_turned")
        out_added = sem("out_added")
        ffn_gate = sem("ffn_gate")
        ffn_mul = sem("ffn_mul")
        ffn_high = sem("ffn_high")
        ffn_low = sem("ffn_low")
        wfin_loaded = sem("wfin_loaded")
        down_taken = sem("down_taken")
        down_turned = sem("down_turned")
        down_added = sem("down_added")
        fin_ready = sem("fin_ready")
        stored = sem("stored")

        block = ctx.enter_context(nc.Block())

        def heads(t):
            return t.unsqueeze(2).broadcast_to([P, t.shape[1], C])

        def half(t, q):
            return t[:, 4 * q:4 * q + 4, :]

        def banks(b, n=1):
            return ps[:, b:b + n, :]

        def bank4(b):
            return ps[:, b, :].rearrange("p (h c) -> p h c", h=4)

        TASKS = [(h, b) for h in range(2) for b in range(TT)]
        START = [h * NS + b * (b + 1) // 2 * P for h, b in TASKS]

        @block.sync
        def _(sp):
            x_tiles = x[0].rearrange("(t p) d -> p t d", p=P)
            for t in range(TT):
                sp.dma_start(x_nat[:, t, :], x_tiles[:, t, :]).then_inc(x_loaded, 16)
            for row, src in ((0, conv_w[0].rearrange("w (n p) -> (w n) p", p=P)),
                             (NMIX, norm_mix_w[0].rearrange("(n p) -> n p", p=P)),
                             (NFFN, norm_ffn_w[0].rearrange("(n p) -> n p", p=P)), (GNW, gdn_norm_w)):
                sp.dma_start(prm_rows[row:row + src.shape[0], :], src).then_inc(prm_loaded, 16)

            def col_tile(wt, col):
                return wt[0].rearrange("(k p) n -> p k n", p=P)[:, :, bass.ds(col, P)]

            def load(q, r, src, first=False):
                if not first:
                    sp.wait_ge(w_low, 4 * q + r - 3)
                sp.dma_start(raw[:, r, :].rearrange("p (k n) -> p k n", n=src.shape[2]), src)\
                    .then_inc(w_loaded[r], 16)

            load(0, 0, col_tile(w_in, 0), True)
            for s in (z_mul, a_merged, b_gated, ffn_low, ffn_mul, z_gate, ma_gate, mb_gate, ffn_gate, out_turned, out_added, a_low, y_low, b_mul, probsT_ready, o_taken, b_low, X_ready, w_done, of_turned, S_done, of_ready, oT_ready, S_ready):
                sp.sem_inc(s, 1)
            w_cols = w_in[0].rearrange("(k p) n -> p k n", p=P)
            sp.dma_start(wsm[:, :, 0:2 * H], w_cols[:, :, GA:GA + 2 * H]).then_inc(small_loaded, 16)
            sp.dma_start(wsm[:, :, 2 * H:32], w_cols[:, :, FF:FF + FH]).then_inc(small_loaded, 16)
            for r in range(1, 4):
                load(0, r, col_tile(w_in, r * P), True)
            sp.wait_ge(x_turned, KT)
            sp.dma_start(bias_dt[:, :], dt_bias[0].partition_broadcast(P)).then_inc(small_loaded, 16)
            sp.dma_start(bias_ff[:, :], fox_f_bias[0].partition_broadcast(P)).then_inc(small_loaded, 16)
            sp.dma_start(alog[:, :], a_log[0].partition_broadcast(P)).then_inc(small_loaded, 16)
            with sp.Fori(1, NCONV // 4) as i:
                for r in range(4):
                    load(i, r, col_tile(w_in, i * (4 * P) + r * P))
            sp.wait_ge(cum_taken, 1)
            sp.dma_start(cum_dram, cum[:, :]).then_inc(cum_stored, 16)
            with sp.Fori(0, H // 4) as i:
                for r in range(4):
                    load(i + Z0, r, col_tile(w_in, i * (4 * P) + (GZ + r * P)))
            with sp.Fori(0, KT // 2) as i:
                for r in range(4):
                    load(i + A0, r, col_tile(w_branch_a, (i + A0) * (2 * P) + (r // 2 - 2 * A0) * P) if r % 2 else
                         col_tile(w_in, i * (2 * P) + (MA + r // 2 * P)))
            with sp.Fori(0, FH // 2) as i:
                for r, col in enumerate((FV, FQ, FK, FO)):
                    load(i + FOX0, r, col_tile(w_in, i * P + col))
            with sp.Fori(0, KT // 2) as i:
                for r in range(4):
                    load(i + B0, r, col_tile(w_branch_b, (i + B0) * (2 * P) + (r // 2 - 2 * B0) * P) if r % 2 else
                         col_tile(w_in, i * (2 * P) + (MB + r // 2 * P)))
            with sp.Fori(0, KT // 4) as i:
                for r in range(4):
                    load(i + OUT0, r, col_tile(w_out, i * (4 * P) + r * P))
            sp.wait_ge(b_low, FH // 2 + 1)
            for t in range(TT):
                sp.dma_start(x_res[:, t, :], x_tiles[:, t, :]).then_inc(xres_loaded, 16)
            with sp.Fori(0, FT // 2) as i:
                for r in range(4):
                    load(i + FFN0, r, col_tile(w_up if r % 2 else w_gate, i * (2 * P) + r // 2 * P))
            down = w_down[0].rearrange("(k p) n -> p k n", p=P)
            sp.wait_ge(out_turned, KT + 1)
            sp.dma_start(wfin[:, :], norm_final_w.partition_broadcast(P)).then_inc(wfin_loaded, 16)
            with sp.Fori(0, FT // 4) as i:
                for r in range(4):
                    load(i + DOWN0, r, down[:, bass.ds(i * 4 + r // 2 * 2, 2), r % 2 * 512:r % 2 * 512 + 512])
            for r in range(2):
                load(DOWN0 + FT // 4, r, down[:, FT - 2:FT, r * 512:r * 512 + 512])
            y_tiles = out[0].rearrange("(t p) d -> p t d", p=P)
            for t in range(TT):
                sp.wait_ge(fin_ready, t + 1)
                sp.dma_start(y_tiles[:, t, :], x_res[:, t, :]).then_inc(stored, 16)
            sp.wait_ge(stored, 16 * TT)

        @block.gpsimd
        def _(pool):
            pool.memset(ident[:, :], 0.0).then_inc(consts_ready, 1)
            pool.memset(step[:, :], 1.0).then_inc(consts_ready, 1)
            pool.memset(after[:, :], 1.0).then_inc(consts_ready, 1)
            pool.memset(low[:, :], 1.0).then_inc(consts_ready, 1)
            pool.memset(pair_neg[:, :], 0.0).then_inc(consts_ready, 1)
            pool.memset(blk_neg[:, :, :], 0.0).then_inc(consts_ready, 1)
            pool.memset(ident_b[:, :], 0.0).then_inc(consts_ready, 1)
            pool.memset(mask_b[:, :], 0.0).then_inc(consts_ready, 1)
            pool.memset(half_neg[:, :], -0.5).then_inc(consts_ready, 1)
            pool.wait_ge(consts_ready, 9)

            def select(t, pattern, base, cm, op, fill):
                return pool.affine_select(out=t, in_=t, compare_op=op, fill=fill, base=base, pattern=pattern,
                                          channel_multiplier=cm)

            select(ident[:, :], [[-1, P]], 0, 1, ALU.not_equal, 1.0).then_inc(consts_ready, 1)
            select(step[:, :], [[1, 7 * P]], -3 * P, -1, ALU.is_ge, 0.0).then_inc(consts_ready, 1)
            select(after[:, :], [[-1, P]], 0, 1, ALU.is_gt, 0.0).then_inc(consts_ready, 1)
            select(low[:, :], [[-1, P]], 0, 1, ALU.is_ge, 0.0).then_inc(consts_ready, 1)
            select(pair_neg[:, :].rearrange("p (r two) -> p r two", two=2)[:, :, 0],
                   [[-2, P // 2]], -1, 1, ALU.not_equal, -1.0).then_inc(consts_ready, 1)
            select(ident_b[:, :], [[-1, P]], 0, 1, ALU.not_equal, 1.0).then_inc(consts_ready, 1)
            select(mask_b[:, :], [[-1, P]], 0, 1, ALU.is_ge, NEG).then_inc(consts_ready, 1)
            for n in range(5):
                s = 2 << n
                v = blk_neg[:, n, :].rearrange("p (r two s) -> p r two s", two=2, s=s)[:, :, 1, :]
                pool.memset(v, -1.0).then_inc(consts_ready, 1)
                pool.wait_ge(consts_ready, 17 + 3 * n)
                select(v, [[-2 * s, P // (2 * s)], [0, s]], 0, 1, ALU.is_ge, 0.0).then_inc(consts_ready, 1)
                pool.wait_ge(consts_ready, 18 + 3 * n)
                select(v, [[2 * s, P // (2 * s)], [0, s]], s - 1, -1, ALU.is_ge, 0.0).then_inc(consts_ready, 1)

            def power(dst, src, n):
                return pool.tensor_tensor(dst, src, half_neg[:, 0:n], ALU.pow)

            def low_part(q, r):
                pool.wait_ge(w_high, 4 * q + r + 1)
                pool.tensor_tensor(w_lo[:, r % 2, :], raw[:, r, :], w_hi[:, r % 2, :], ALU.subtract)\
                    .then_inc(w_low, 1)

            def units(first, n):
                with pool.Fori(0, n) as i:
                    for r in range(4):
                        low_part(i + first, r)

            pool.wait_ge(ms_ready, 1)
            power(rstd[:, :], ms[:, :], TT).then_inc(rstd_ready, 1)
            units(QKV0, NCONV // 4)
            pool.wait_ge(state_zero, 1)
            with pool.Fori(0, TT) as c:
                pool.wait_ge(X_ready, c * 8 + 1)
                pool.wait_ge(w_done, c * 2 + 1)
                pool.tensor_tensor(gm[:, :, :], after[:, :].unsqueeze(1).broadcast_to([P, H, C]),
                                   heads(g[:, bass.ds(c * H, H)]), ALU.mult).then_inc(gm_ready, 1)
                pool.wait_ge(sums_taken, c + 1)
                power(rn[:, :], nsum[:, :], 2 * H).then_inc(rn_ready, 1)
                pool.wait_ge(E_masked, c + 1)
                pool.wait_ge(row_step, c * 3 + 2)
                pool.wait_ge(D_done, c * 2 + 2)
                pool.tensor_tensor(Eb[:, :, :], E[:, :, :], heads(bn2[:, :]), ALU.mult).then_inc(Eb_ready, 1)
                pool.wait_ge(osc_step, c * 4 + 3)
                power(osc[:, :], oss[:, :], H).then_inc(osc_pow, 1)
            units(Z0, FFN0 - Z0)
            pool.wait_ge(ms_ready, 2)
            power(rstd[:, :], ms[:, :], TT).then_inc(rstd_ready, 1)
            units(FFN0, DOWN0 + FT // 4 - FFN0)
            for r in range(2):
                low_part(DOWN0 + FT // 4, r)
            pool.wait_ge(ms_ready, 3)
            power(rstd[:, :], ms[:, :], TT).then_inc(rstd_ready, 1)

        @block.scalar
        def _(act):
            def high_part(q, r, first=False):
                act.wait_ge(w_loaded[r], 16 * q + 16)
                if not first:
                    act.wait_ge(unit_done, 4 * q + r - 1)
                act.activation(w_hi[:, r % 2, :], raw[:, r, :], ACT.Copy).then_inc(w_high, 1)

            def next_high(q, r):
                if r < 3:
                    high_part(q, r + 1)
                else:
                    high_part(q + 1, 0)

            def squares(src, junk):
                for t in range(TT):
                    act.activation(junk[:, t, :], src[:, t, :], ACT.Square,
                                   accum_out=ss[:, t:t + 1]).then_inc(sq_summed, 1)

            def norm_high(n, col):
                for k in range(KT):
                    act.wait_ge(x_turned, KT * n + k + 1)
                    act.activation(h_hi[:, k, :], banks(k % 4)[:, 0, :], ACT.Copy,
                                   scale=prm[:, col + k:col + k + 1]).then_inc(h_high, 1)

            act.wait_ge(x_loaded, 16 * TT)
            squares(x_nat, xn)
            act.wait_ge(prm_turned, 1)
            act.activation(prm[:, :], ps[:, 7, 0:NPRM], ACT.Copy).then_inc(prm_ready, 1)
            high_part(0, 0, True)
            act.wait_ge(prm_ready, 1)
            norm_high(0, NMIX)

            act.wait_ge(small_taken, 3)
            act.activation(gabs[:, :, :], gv[:, :, :], ACT.Abs).then_inc(gate_exp, 1)
            act.wait_ge(gate_exp, 1)
            act.activation(gabs[:, :, :], gabs[:, :, :], ACT.Exp, scale=-1.0).then_inc(gate_exp, 1)
            act.activation(gb[:, :, :], gb[:, :, :], ACT.Exp, scale=-1.0).then_inc(gate_exp, 1)
            act.wait_ge(small_loaded, 16 * 5)
            act.activation(alog[:, :], alog[:, :], ACT.Exp).then_inc(gate_exp, 1)
            act.wait_ge(gate_exp, 2)
            act.activation(gabs[:, :, :], gabs[:, :, :], ACT.Ln, bias=1.0).then_inc(gate_exp, 1)
            act.wait_ge(gate_sums, 1)
            act.activation(gexp[:, :, :], ps[:, 5, 0:3 * TT * H].rearrange("p (a n) -> p a n", a=3),
                           ACT.Exp).then_inc(gexp_ready, 1)
            act.wait_ge(gate_sums, 2)
            act.activation(cum[:, :], ps[0:FH, 6, :], ACT.Copy).then_inc(cum_taken, 1)

            def conv(q, r, first=False):
                if r == 0 and first:
                    high_part(0, 1, True)
                else:
                    next_high(q, r)
                act.wait_ge(unit_done, 4 * q + r + 1)
                if not (first and r < 2):
                    act.wait_ge(conv_out, 4 * q + r - 1)
                act.activation(cv[:, r % 2, :], ps[:, r, :], ACT.Copy,
                               scale=prm[:, bass.ds(4 * q + (3 * NCONV + r), 1)]).then_inc(conv_seed, 1)
                act.wait_ge(conv_tap, 12 * q + 3 * r + 3)
                act.activation(qkv[:, bass.ds(4 * q + r, 1), :], cv[:, r % 2:r % 2 + 1, :], ACT.Silu)\
                    .then_inc(conv_out, 1)

            for r in range(4):
                conv(0, r, True)
            with act.Fori(1, NCONV // 4) as i:
                for r in range(4):
                    conv(i, r)

            act.wait_ge(conv_out, NCONV)
            with act.Fori(0, TT) as c:
                cols = bass.ds(c * C, C)
                act.wait_ge(of_turned, c * 2 + 1)
                act.activation(sq[:, :, :], qkv[:, 0:2 * H, cols], ACT.Square).then_inc(squared, 1)
                act.activation(kS[:, :, :], qkv[:, H:2 * H, cols], ACT.Copy).then_inc(staged, 1)
                act.activation(qS[:, :, :], qkv[:, 0:H, cols], ACT.Copy).then_inc(staged, 1)
                act.wait_ge(D_done, c * 2 + 2)
                act.wait_ge(S_done, c * 2 + 1)
                act.activation(E[:, :, :].rearrange("p h c -> p (h c)"),
                               banks(0, 2).rearrange("p b n -> p (b n)"), ACT.Exp).then_inc(E_exp, 1)
                for a in range(2):
                    act.wait_ge(Z_turned, c * 2 + a + 1)
                    act.activation(half(Zm, a), bank4(2 + a), ACT.Copy).then_inc(Z_ready, 1)
                for a in range(2):
                    act.wait_ge(qk_turned, c * 2 + a + 1)
                    act.activation(half(qkT, a), bank4(4 + a), ACT.Copy).then_inc(qkT_ready, 1)
                for a in range(2):
                    act.wait_ge(Y_done, c * 12 + 10 + a + 1)
                    act.activation(half(Yn, a)[0:64, :, 64:P], bank4(6 + a)[0:64, :, 64:P], ACT.Copy,
                                   scale=-1.0).then_inc(Y_ready, 1)
                for a in range(2):
                    act.wait_ge(ZT_done, c * 12 + 10 + a + 1)
                    act.activation(half(Zm, a)[0:64, :, 64:P], bank4(a)[0:64, :, 64:P], ACT.Copy)\
                        .then_inc(Z_ready, 1)
                for h in range(H):
                    act.wait_ge(qs_done, c * 2 + h // 4 + 1)
                    act.activation(o[:, h, :], bank4(6 + h // 4)[:, h % 4, :], ACT.Copy,
                                   scale=gexp[:, 0, bass.ds(c * H + h, 1)]).then_inc(qs_ready, 1)
                for a in range(2):
                    act.wait_ge(w_done, c * 2 + a + 1 + 1)
                    act.activation(half(w, a), bank4(a), ACT.Copy).then_inc(w_ready, 1)
                for h in range(H):
                    act.wait_ge(o_ready, c * 2 + h // 4 + 1)
                    act.activation(of[:, h, :], o[:, h, :], ACT.Square,
                                   accum_out=oss[:, h:h + 1]).then_inc(o_squared, 1)
                for a in range(2):
                    act.wait_ge(of_turned, c * 2 + a + 1 + 1)
                    act.activation(mixT[:, 4 * a:4 * a + 4, cols], bank4(6 + a), ACT.Copy).then_inc(oT_ready, 1)

            with act.Fori(0, H // 4) as i:
                for r in range(4):
                    next_high(i + Z0, r)
                    act.wait_ge(unit_done, (i + Z0) * 4 + r + 1)
                    act.wait_ge(z_mul, i * 4 + r + 1)
                    act.activation(gate[:, r % 2, :], ps[:, r, :], ACT.Silu).then_inc(z_gate, 1)

            def merge_gates(first, n, func, done, merged):
                with act.Fori(0, n) as i:
                    for r in range(4):
                        next_high(i + first, r)
                        if r % 2 == 0:
                            act.wait_ge(unit_done, (i + first) * 4 + r + 1)
                            act.wait_ge(merged, i * 2 + 1)
                            act.activation(gate[:, r // 2, :], ps[:, r, :], func).then_inc(done, 1)

            act.wait_ge(z_mul, H + 1)
            merge_gates(A0, KT // 2, ACT.Sigmoid, ma_gate, a_merged)

            def fox(i, products, attention):
                if products:
                    next_high(i + FOX0, 0)
                if attention:
                    for t, (h, b) in enumerate(TASKS):
                        act.wait_ge(score_taken, 8 * i - 8 + t + 1)
                        s = probs[:, START[t]:START[t] + (b + 1) * P]
                        act.activation(s, s, ACT.Exp, bias=nmax[:, t:t + 1], scale=-1.0,
                                       accum_out=psum_p[:, t:t + 1]).then_inc(probs_ready, 1)
                if products:
                    if i is 0:
                        act.wait_ge(cum_stored, 16)
                    act.dma_start(cumb[:, :, :], cum_dram[bass.ds(2 * i, 2), :].partition_broadcast(P))\
                        .then_inc(cumb_loaded, 16)
                    act.wait_ge(unit_done, (i + FOX0) * 4 + 1)
                    act.wait_ge(v_back, i)
                    act.activation(vT[:, :], ps[:, 0, :], ACT.Copy).then_inc(v_taken, 1)
                    next_high(i + FOX0, 1)
                    act.wait_ge(unit_done, (i + FOX0) * 4 + 2)
                    for h in range(2):
                        act.activation(qx[:, h, :], ps[h * FD:(h + 1) * FD, 1, :], ACT.Copy,
                                       scale=FD ** -0.5).then_inc(q_taken, 1)
                    next_high(i + FOX0, 2)
                    next_high(i + FOX0, 3)
                    act.wait_ge(unit_done, (i + FOX0) * 4 + 4)
                    if attention:
                        act.wait_ge(fo_step, 2 * i)
                    act.activation(efo[:, :], ps[:, 3, :], ACT.Exp, scale=-1.0).then_inc(fo_exp, 1)

            fox(0, True, False)
            with act.Fori(1, FH // 2) as i:
                fox(i, True, True)
            fox(FH // 2, False, True)

            act.wait_ge(a_merged, KT + 1)
            merge_gates(B0, KT // 2, ACT.Sigmoid, mb_gate, b_gated)

            with act.Fori(0, KT // 4) as i:
                for r in range(4):
                    next_high(i + OUT0, r)
                    act.wait_ge(unit_done, (i + OUT0) * 4 + r + 1)
                    if r < 2:
                        act.wait_ge(out_turned, i * 4 + 1)
                    else:
                        act.wait_ge(out_turned, i * 4 + r - 1 + 1)
                    act.activation(back[:, r % 2, :], ps[:, r, :], ACT.Copy).then_inc(out_taken, 1)

            act.wait_ge(out_added, KT + 1)
            squares(x_res, xn2)
            norm_high(1, NFFN)
            merge_gates(FFN0, FT // 2, ACT.Silu, ffn_gate, ffn_low)

            with act.Fori(0, FT // 4) as i:
                for r in range(4):
                    next_high(i + DOWN0, r)
            high_part(DOWN0 + FT // 4, 1)
            for j in range(KT):
                act.wait_ge(unit_done, 4 * (DOWN0 + FT // 4) + j // 4 + 1)
                if j >= 2:
                    act.wait_ge(down_turned, j - 1)
                act.activation(back[:, j % 2, :], ps[:, j, :], ACT.Copy).then_inc(down_taken, 1)
            for t in range(TT):
                act.wait_ge(down_added, KT)
                act.activation(raw[:, t, :], x_res[:, t, :], ACT.Square,
                               accum_out=ss[:, t:t + 1]).then_inc(sq_summed, 1)

        @block.vector
        def _(dve):
            def copy(dst, src):
                return dve.tensor_copy(dst, src)

            def rms(n, src, dst):
                dve.wait_ge(sq_summed, TT * (n + 1))
                dve.tensor_scalar(ms[:, :], ss[:, :], 1.0 / D, EPS, ALU.mult, ALU.add).then_inc(ms_ready, 1)
                dve.wait_ge(rstd_ready, n + 1)
                for t in range(TT if dst is not None else 0):
                    dve.tensor_scalar(dst[:, t, :], src[:, t, :], rstd[:, t:t + 1], None,
                                      ALU.mult).then_inc(x_scaled, 1)

            def norm_low(n, col):
                for k in range(KT):
                    dve.wait_ge(h_high, KT * n + k + 1)
                    dve.scalar_tensor_tensor(out=h_lo[:, k, :], in0=ps[:, k % 4, :],
                                             scalar=prm[:, col + k:col + k + 1],
                                             in1=h_hi[:, k, :].bitcast(F32), op0=ALU.mult,
                                             op1=ALU.subtract).then_inc(h_low, 1)

            rms(0, x_nat, xn)
            dve.wait_ge(small_loaded, 32)
            copy(wsm_hi[:, :, :], wsm[:, :, :]).then_inc(wsm_high, 1)
            dve.wait_ge(wsm_high, 1)
            dve.tensor_tensor(wsm_lo[:, :, :], wsm[:, :, :], wsm_hi[:, :, :].bitcast(F32), ALU.subtract)\
                .then_inc(wsm_ready, 1)
            norm_low(0, NMIX)

            small = ps[:, 4, 0:TT * 32].rearrange("p (t n) -> p t n", t=TT)
            dve.wait_ge(small_done, 1)
            dve.wait_ge(small_loaded, 16 * 5)
            dve.tensor_tensor(gv[:, :, 0:H], small[:, :, 0:H],
                              bias_dt[:, :].unsqueeze(1).broadcast_to([P, TT, H]), ALU.add)\
                .then_inc(small_taken, 1)
            dve.scalar_tensor_tensor(out=gv[:, :, H:3 * H], in0=small[:, :, 2 * H:32], scalar=-1.0,
                                     in1=bias_ff[:, :].unsqueeze(1).broadcast_to([P, TT, FH]),
                                     op0=ALU.mult, op1=ALU.subtract).then_inc(small_taken, 1)
            copy(gb[:, :, :], small[:, :, H:2 * H]).then_inc(small_taken, 1)
            dve.wait_ge(gate_exp, 5)
            dve.scalar_tensor_tensor(out=sp[:, :, :], in0=gv[:, :, :], scalar=0.0, in1=gabs[:, :, :],
                                     op0=ALU.max, op1=ALU.add).then_inc(gate_step, 1)
            dve.tensor_scalar(gb[:, :, :], gb[:, :, :], 1.0, None, ALU.add).then_inc(gate_step, 1)
            dve.wait_ge(gate_step, 2)
            dve.reciprocal(beta[:, :].rearrange("p (t h) -> p t h", t=TT), gb[:, :, :]).then_inc(gate_step, 1)
            dve.scalar_tensor_tensor(out=g[:, :].rearrange("p (t h) -> p t h", t=TT), in0=sp[:, :, 0:H],
                                     scalar=-1.0, in1=alog[:, :].unsqueeze(1).broadcast_to([P, TT, H]),
                                     op0=ALU.mult, op1=ALU.mult).then_inc(gate_step, 1)

            with dve.Fori(0, NCONV // 4) as i:
                for r in range(4):
                    dve.wait_ge(conv_seed, i * 4 + r + 1)
                    for n in range(1, TAPS):
                        if n > 1:
                            dve.wait_ge(conv_tap, i * 12 + 3 * r + n - 1)
                        ins = dve.scalar_tensor_tensor(
                            out=cv[:, r % 2, n:T], in0=ps[:, r, 0:T - n],
                            scalar=prm[:, bass.ds(i * 4 + ((TAPS - 1 - n) * NCONV + r), 1)],
                            in1=cv[:, r % 2, n:T], op0=ALU.mult, op1=ALU.add)
                        ins.then_inc(conv_tap, 1)
                    dve.wait_ge(conv_tap, i * 12 + 3 * r + 3)
                    dve.sem_inc(conv_bank, 1)

            dve.memset(S[:, :, :], 0.0).then_inc(state_zero, 1)
            dve.wait_ge(state_zero, 1)
            dve.wait_ge(gexp_ready, 1)
            dve.wait_ge(conv_out, NCONV)
            with dve.Fori(0, TT) as c:
                cols = bass.ds(c * C, C)
                hc = bass.ds(c * H, H)
                dve.wait_ge(of_ready, c + 1)
                copy(vS[:, :, :], qkv[:, 2 * H:3 * H, cols]).then_inc(staged, 1)
                dve.wait_ge(sums_done, c + 1)
                dve.tensor_scalar(nsum[:, :], ps[:, 7, 0:2 * H], EPS, None, ALU.add).then_inc(sums_taken, 1)
                dve.wait_ge(rn_ready, c + 1)
                dve.tensor_tensor(bn[:, :], beta[:, hc], rn[:, H:2 * H], ALU.mult).then_inc(row_step, 1)
                dve.wait_ge(row_step, c * 3 + 1)
                dve.tensor_tensor(bn2[:, :], bn[:, :], rn[:, H:2 * H], ALU.mult).then_inc(row_step, 1)
                dve.wait_ge(row_step, c * 3 + 2)
                dve.scalar_tensor_tensor(out=c1[:, :], in0=bn2[:, :], scalar=-1.0, in1=gexp[:, 0, hc],
                                         op0=ALU.mult, op1=ALU.mult).then_inc(row_step, 1)
                dve.wait_ge(E_exp, c + 1)
                dve.tensor_tensor(E[:, :, :], E[:, :, :], low[:, :].unsqueeze(1).broadcast_to([P, H, C]),
                                  ALU.mult).then_inc(E_masked, 1)
                for a in range(2):
                    dve.wait_ge(k_turned, c * 2 + a + 1)
                    dve.tensor_tensor(half(Kd, a), bank4(2 + a),
                                      heads(gexp[:, 1, bass.ds(c * H + 4 * a, 4)]), ALU.mult)\
                        .then_inc(Kd_ready, 1)
                for a in range(2):
                    dve.wait_ge(v_turned, c * 2 + a + 1)
                    dve.tensor_tensor(half(Vb, a), bank4(4 + a), heads(bn[:, 4 * a:4 * a + 4]), ALU.mult)\
                        .then_inc(Vb_ready, 1)
                dve.wait_ge(Eb_ready, c + 1)
                for a in range(2):
                    dve.wait_ge(G_done, c * 2 + a + 1)
                    dve.tensor_tensor(half(L, a), bank4(6 + a), half(Eb, a), ALU.mult).then_inc(L_ready, 1)
                    dve.wait_ge(L_ready, c * 2 + a + 1)
                    dve.tensor_tensor(half(Tm, a), half(L, a), pair_neg[:, :].unsqueeze(1)
                                      .broadcast_to([P, 4, C]), ALU.mult).then_inc(T_step, 1)
                    dve.wait_ge(T_step, c * 4 + 2 * a + 1)
                    dve.tensor_tensor(half(Tm, a), half(Tm, a), ident[:, :].unsqueeze(1)
                                      .broadcast_to([P, 4, C]), ALU.add).then_inc(T_step, 1)
                dve.wait_ge(E_masked, c + 1)
                for a in range(2):
                    dve.wait_ge(qk_done, c * 2 + a + 1)
                    dve.tensor_tensor(half(qk, a), bank4(a), half(E, a), ALU.mult).then_inc(qk_ready, 1)
                for n in range(5):
                    for a in range(2):
                        dve.wait_ge(Y_done, c * 12 + 2 * n + a + 1)
                        dve.tensor_tensor(half(Yn, a), bank4(6 + a), blk_neg[:, n:n + 1, :]
                                          .broadcast_to([P, 4, C]), ALU.mult).then_inc(Y_ready, 1)
                    for a in range(2):
                        dve.wait_ge(ZT_done, c * 12 + 2 * n + a + 1)
                        if n == 0:
                            dve.wait_ge(Z_ready, c * 4 + a + 1)
                        dve.tensor_tensor(half(Zm, a), half(Zm, a), bank4(a), ALU.add).then_inc(ZT_ready, 1)
                        dve.tensor_tensor(half(Tm, a), half(Tm, a), bank4(2 + a), ALU.add).then_inc(ZT_ready, 1)
                        if n < 4:
                            dve.wait_ge(ZT_ready, c * 20 + 4 * n + 2 * a + 2)
                dve.wait_ge(Vb_ready, c * 2 + 2)
                dve.wait_ge(row_step, c * 3 + 3)
                for h in range(H):
                    dve.wait_ge(ks_done, c * 2 + h // 4 + 1)
                    dve.scalar_tensor_tensor(out=X[:, h, :], in0=bank4(4 + h // 4)[:, h % 4, :],
                                             scalar=c1[:, h:h + 1], in1=Vb[:, h, :], op0=ALU.mult,
                                             op1=ALU.add).then_inc(X_ready, 1)
                for a in range(2):
                    dve.wait_ge(qkw_done, c * 2 + a + 1)
                    dve.wait_ge(qs_ready, c * 8 + 4 * a + 4)
                    dve.tensor_tensor(half(o, a), half(o, a), bank4(2 + a), ALU.add).then_inc(o_ready, 1)
                for h in range(H):
                    dve.wait_ge(S_done, c * 2 + h // 4 + 1 + 1)
                    dve.scalar_tensor_tensor(out=S[:, h, :], in0=S[:, h, :],
                                             scalar=gexp[:, 2, bass.ds(c * H + h, 1)],
                                             in1=bank4(4 + h // 4)[:, h % 4, :], op0=ALU.mult,
                                             op1=ALU.add).then_inc(S_ready, 1)
                dve.wait_ge(o_squared, c * 8 + 8)
                dve.tensor_tensor(oss[:, :], oss[:, :], rn[:, 0:H], ALU.mult).then_inc(osc_step, 1)
                dve.wait_ge(osc_step, c * 4 + 1)
                dve.tensor_tensor(oss[:, :], oss[:, :], rn[:, 0:H], ALU.mult).then_inc(osc_step, 1)
                dve.wait_ge(osc_step, c * 4 + 2)
                dve.tensor_scalar(oss[:, :], oss[:, :], 1.0 / (DK * DK), EPS, ALU.mult, ALU.add)\
                    .then_inc(osc_step, 1)
                dve.wait_ge(osc_pow, c + 1)
                dve.scalar_tensor_tensor(out=osc[:, :], in0=osc[:, :], scalar=DK ** -0.5, in1=rn[:, 0:H],
                                         op0=ALU.mult, op1=ALU.mult).then_inc(osc_step, 1)
                dve.wait_ge(osc_step, c * 4 + 4)
                dve.wait_ge(o_ready, c * 2 + 2)
                dve.tensor_tensor(of[:, :, :], o[:, :, :], heads(osc[:, :]), ALU.mult).then_inc(of_ready, 1)

            def split(hi, lo, src, high, low_, n):
                copy(hi, src).then_inc(high, 1)
                dve.wait_ge(high, n + 1)
                dve.tensor_tensor(lo, src, hi.bitcast(F32), ALU.subtract).then_inc(low_, 1)

            dve.wait_ge(oT_ready, 2 * TT + 1)
            dve.wait_ge(prm_ready, 1)
            with dve.Fori(0, H // 4) as i:
                for r in range(4):
                    dve.wait_ge(z_gate, i * 4 + r + 1 + 1)
                    if r < 2:
                        dve.wait_ge(a_low, i * 4 + 1)
                    else:
                        dve.wait_ge(a_low, i * 4 + r - 1 + 1)
                    dve.scalar_tensor_tensor(out=tmp[:, r % 2, :], in0=mixT[:, bass.ds(i * 4 + r, 1), :],
                                             scalar=prm[:, GNW:GNW + 1], in1=gate[:, r % 2, :], op0=ALU.mult,
                                             op1=ALU.mult).then_inc(z_mul, 1)
                    dve.wait_ge(z_mul, i * 4 + r + 1 + 1)
                    split(a_hi[:, bass.ds(i * 4 + r, 1), :], a_lo[:, bass.ds(i * 4 + r, 1), :],
                          tmp[:, r % 2:r % 2 + 1, :], a_high, a_low, i * 4 + r)
            with dve.Fori(0, KT // 2) as i:
                for r in range(2):
                    dve.wait_ge(unit_done, (i + A0) * 4 + 2 * r + 2)
                    dve.wait_ge(ma_gate, i * 2 + r + 1 + 1)
                    dve.tensor_tensor(mixT[:, bass.ds(i * 2 + r, 1), :], gate[:, r:r + 1, :],
                                      ps[:, 2 * r + 1:2 * r + 2, :], ALU.mult).then_inc(a_merged, 1)

            def fox(i, products, attention):
                if attention:
                    for t, (h, b) in enumerate(TASKS):
                        if t == 0:
                            dve.wait_ge(cumb_loaded, 16 * i)
                        dve.wait_ge(score_done, 8 * i - 8 + t + 1)
                        dve.memset(scratch[:, t:t + 1], 0.0)
                        n = (b + 1) * P
                        dve.tensor_tensor_reduce(probs[:, START[t]:START[t] + n], ps[:, 4 + t % 3, 0:n],
                                                 cumb[:, h, 0:n], -1.0, 3.0e38, ALU.add, ALU.min,
                                                 nmax[:, t:t + 1]).then_inc(score_taken, 1)
                    for t, (h, b) in enumerate(TASKS):
                        dve.wait_ge(probs_turned, 8 * i - 8 + t + 1)
                        n = (b + 1) * P
                        copy(probsT[:, START[t]:START[t] + n], ps[:, 4 + t % 3, 0:n]).then_inc(probsT_ready, 1)
                    dve.wait_ge(probs_ready, 8 * i)
                    dve.reciprocal(rsum[:, :], psum_p[:, :]).then_inc(rsum_ready, 1)
                    dve.wait_ge(fo_exp, i)
                    dve.tensor_scalar(sfo[:, :], efo[:, :], 1.0, None, ALU.add).then_inc(fo_step, 1)
                    dve.wait_ge(fo_step, 2 * i - 1)
                    dve.reciprocal(sfo[:, :], sfo[:, :]).then_inc(fo_step, 1)
                    dve.wait_ge(rsum_ready, i)
                    dve.wait_ge(pv_done, i)
                    for h in range(2):
                        dve.tensor_tensor(
                            o_nat[:, :, h * FD:(h + 1) * FD],
                            ps[:, 7, :].rearrange("p (h b d) -> p h b d", h=2, b=TT)[:, h],
                            rsum[:, h * TT:(h + 1) * TT].unsqueeze(2).broadcast_to([P, TT, FD]),
                            ALU.mult).then_inc(o_taken, 1)
                if products:
                    dve.wait_ge(unit_done, (i + FOX0) * 4 + 3)
                    for h in range(2):
                        copy(kx[:, h, :], ps[h * FD:(h + 1) * FD, 2, :]).then_inc(k_taken, 1)
                if attention:
                    dve.wait_ge(o_turned, i)
                    dve.wait_ge(fo_step, 2 * i)
                    if not (i is 1):
                        dve.wait_ge(b_low, i - 1 + 1)
                    dve.tensor_tensor(tmp[:, 0, :], ps[:, 4, :], sfo[:, :], ALU.mult).then_inc(b_mul, 1)
                    dve.wait_ge(b_mul, i + 1)
                if products:
                    dve.wait_ge(v_back, i + 1)
                    copy(v_nat[:, :, :], ps[:, 5, :].rearrange("p (t n) -> p t n", t=TT)).then_inc(v_ready, 1)
                if attention:
                    split(b_hi[:, bass.ds(i - 1, 1), :], b_lo[:, bass.ds(i - 1, 1), :], tmp[:, 0:1, :],
                          b_high, b_low, i - 1)

            dve.wait_ge(a_low, H + 1)
            fox(0, True, False)
            with dve.Fori(1, FH // 2) as i:
                fox(i, True, True)
            fox(FH // 2, False, True)

            dve.wait_ge(b_low, FH // 2 + 1)
            dve.wait_ge(a_merged, KT + 1)
            with dve.Fori(0, KT // 2) as i:
                for r in range(2):
                    j = i * 2 + r
                    row = bass.ds(j, 1)
                    dve.wait_ge(unit_done, (i + B0) * 4 + 2 * r + 2)
                    dve.wait_ge(mb_gate, j + 1 + 1)
                    if r == 0:
                        dve.wait_ge(y_low, i * 2 + 1)
                    dve.tensor_tensor(tmp[:, r:r + 1, :], gate[:, r:r + 1, :], ps[:, 2 * r + 1:2 * r + 2, :],
                                      ALU.mult).then_inc(b_gated, 1)
                    dve.wait_ge(b_gated, j + 1 + 1)
                    dve.tensor_tensor(tmp[:, r:r + 1, :], tmp[:, r:r + 1, :], mixT[:, row, :], ALU.add)\
                        .then_inc(y_sum, 1)
                    dve.wait_ge(y_sum, j + 1)
                    split(a_hi[:, row, :], a_lo[:, row, :], tmp[:, r:r + 1, :], y_high, y_low, j)

            dve.wait_ge(xres_loaded, 16 * TT)
            with dve.Fori(0, KT // 4) as i:
                for r in range(4):
                    cols = bass.ds(i * (4 * P) + r * P, P)
                    dve.wait_ge(out_turned, i * 4 + r + 1 + 1)
                    dve.tensor_tensor(x_res[:, :, cols], x_res[:, :, cols],
                                      ps[:, 4 + r % 2, :].rearrange("p (t n) -> p t n", t=TT), ALU.add)\
                        .then_inc(out_added, 1)
            rms(1, x_res, xn2)
            norm_low(1, NFFN)
            with dve.Fori(0, FT // 2) as i:
                for r in range(2):
                    j = i * 2 + r
                    row = bass.ds(j, 1)
                    dve.wait_ge(unit_done, (i + FFN0) * 4 + 2 * r + 2)
                    dve.wait_ge(ffn_gate, j + 1 + 1)
                    if r == 0:
                        dve.wait_ge(ffn_low, i * 2 + 1)
                    dve.tensor_tensor(tmp[:, r:r + 1, :], gate[:, r:r + 1, :], ps[:, 2 * r + 1:2 * r + 2, :],
                                      ALU.mult).then_inc(ffn_mul, 1)
                    dve.wait_ge(ffn_mul, j + 1 + 1)
                    split(f_hi[:, row, :], f_lo[:, row, :], tmp[:, r:r + 1, :], ffn_high, ffn_low, j)

            for j in range(KT):
                dve.wait_ge(down_turned, j + 1)
                dve.tensor_tensor(x_res[:, :, j * P:(j + 1) * P], x_res[:, :, j * P:(j + 1) * P],
                                  ps[:, j, :].rearrange("p (t n) -> p t n", t=TT), ALU.add)\
                    .then_inc(down_added, 1)
            rms(2, x_res, None)
            dve.wait_ge(wfin_loaded, 16)
            for t in range(TT):
                dve.scalar_tensor_tensor(out=x_res[:, t, :], in0=x_res[:, t, :], scalar=rstd[:, t:t + 1],
                                         in1=wfin[:, :], op0=ALU.mult, op1=ALU.mult).then_inc(fin_ready, 1)

        @block.tensor
        def _(pe):
            def turn(dst, src, idn=ident):
                return pe.transpose(dst, src, idn[:src.shape[0], :src.shape[0]])

            def turn_rows(n, src):
                for k in range(KT):
                    if k >= 4:
                        pe.wait_ge(h_low, KT * n + k - 3)
                    for t in range(TT):
                        if k == 0:
                            pe.wait_ge(x_scaled, TT * n + t + 1)
                        last = turn(ps[:, k % 4, t * P:(t + 1) * P], src[:, t, k * P:(k + 1) * P])
                    last.then_inc(x_turned, 1)

            def unit(q, r, hi, lo, tasks=()):
                pe.wait_ge(w_low, 4 * q + r + 1)
                tasks = list(tasks)
                n, every = 0, max(1, 3 * KT // max(1, len(tasks)))
                for wt, xt in ((w_hi, hi), (w_hi, lo), (w_lo, hi)):
                    for k in range(KT):
                        if tasks and n % every == every - 1:
                            tasks.pop(0)()
                        last = pe.matmul(ps[:, r, :], wt[:, r % 2, k * P:(k + 1) * P], xt[:, k, :],
                                         start=(n == 0), stop=(n == 3 * KT - 1))
                        n += 1
                last.then_inc(unit_done, 1)
                for task in tasks:
                    task()

            pe.wait_ge(consts_ready, 31)
            pe.wait_ge(prm_loaded, 64)
            turn(ps[:, 7, 0:NPRM], prm_rows[0:NPRM, :]).then_inc(prm_turned, 1)
            turn_rows(0, xn)

            pe.wait_ge(wsm_ready, 1)
            pe.wait_ge(h_low, KT)
            for t in range(TT):
                n = 0
                for xt, wt in ((h_hi, wsm_hi), (h_lo, wsm_hi), (h_hi, wsm_lo)):
                    for k in range(KT):
                        last = pe.matmul(ps[:, 4, t * 32:(t + 1) * 32], xt[:, k, t * P:(t + 1) * P],
                                         wt[:, k, :], start=(n == 0), stop=(n == 3 * KT - 1))
                        n += 1
            last.then_inc(small_done, 1)

            def gate_sum():
                pe.wait_ge(gate_step, 4)
                for n, lhs in enumerate((step[:, 3 * P:4 * P], after[:, :], step[:, 4 * P:5 * P])):
                    last = pe.matmul(ps[:, 5, n * TT * H:(n + 1) * TT * H], lhs, g[:, :], start=True, stop=True)
                last.then_inc(gate_sums, 1)
                for t in range(TT):
                    last = pe.matmul(ps[0:FH, 6, :], sp[:, t, H:3 * H], step[:, (3 - t) * P:(3 - t) * P + T],
                                     start=(t == 0), stop=(t == TT - 1))
                last.then_inc(gate_sums, 1)

            pe.sem_inc(conv_bank, 4)
            for r in range(4):
                pe.wait_ge(conv_bank, r + 1)
                unit(0, r, h_hi, h_lo)
                if r == 0:
                    gate_sum()
            with pe.Fori(1, NCONV // 4) as i:
                for r in range(4):
                    pe.wait_ge(conv_bank, i * 4 + r + 1)
                    unit(i, r, h_hi, h_lo)

            pe.wait_ge(conv_tap, 3 * NCONV)
            pe.wait_ge(gexp_ready, 1)
            pe.wait_ge(cum_taken, 1)
            with pe.Fori(0, TT) as c:
                ones = step[:, 4 * P:4 * P + 1]
                pe.wait_ge(squared, c + 1)
                pe.wait_ge(oT_ready, c * 2 + 1)
                for h in range(2 * H):
                    last = pe.matmul(ps[:, 7, h:h + 1], sq[:, h, :], ones, start=True, stop=True)
                last.then_inc(sums_done, 1)
                pe.wait_ge(gm_ready, c + 1)
                for a in range(2):
                    pe.matmul(ps[:, a, :], step[:, 3 * P:4 * P], half(gm, a).rearrange("p h c -> p (h c)"),
                              start=True, stop=True).then_inc(D_done, 1)
                pe.wait_ge(staged, c * 3 + 3)
                for a in range(2):
                    for h in range(4):
                        last = turn(bank4(2 + a)[:, h, :], kS[:, 4 * a + h, :])
                    last.then_inc(k_turned, 1)
                pe.wait_ge(S_ready, c * 8 + 1)
                for a in range(2):
                    for h in range(4):
                        last = turn(bank4(4 + a)[:, h, :], vS[:, 4 * a + h, :])
                    last.then_inc(v_turned, 1)
                pe.wait_ge(sums_taken, c + 1)
                for a in range(2):
                    for h in range(4):
                        last = pe.matmul(bank4(6 + a)[:, h, :], kS[:, 4 * a + h, :], kS[:, 4 * a + h, :],
                                         start=True, stop=True)
                    last.then_inc(G_done, 1)
                pe.wait_ge(E_exp, c + 1)
                for a in range(2):
                    for h in range(4):
                        last = pe.matmul(bank4(a)[:, h, :], qS[:, 4 * a + h, :], kS[:, 4 * a + h, :],
                                         start=True, stop=True)
                    last.then_inc(qk_done, 1)
                for a in range(2):
                    pe.wait_ge(T_step, c * 4 + 2 * a + 2)
                    pe.wait_ge(Kd_ready, c * 2 + a + 1)
                    for h in range(4):
                        last = turn(bank4(2 + a)[:, h, :], Tm[:, 4 * a + h, :])
                    last.then_inc(Z_turned, 1)
                for a in range(2):
                    pe.wait_ge(qk_ready, c * 2 + a + 1)
                    pe.wait_ge(Vb_ready, c * 2 + a + 1)
                    for h in range(4):
                        last = turn(bank4(4 + a)[:, h, :], qk[:, 4 * a + h, :])
                    last.then_inc(qk_turned, 1)
                for n in range(5):
                    for a in range(2):
                        if n == 0:
                            pe.wait_ge(Z_ready, c * 4 + a + 1)
                        else:
                            pe.wait_ge(ZT_ready, c * 20 + 4 * n + 2 * a - 2)
                        for h in range(4):
                            last = pe.matmul(bank4(6 + a)[:, h, :], L[:, 4 * a + h, :], Zm[:, 4 * a + h, :],
                                             start=True, stop=True)
                        last.then_inc(Y_done, 1)
                    for a in range(2):
                        pe.wait_ge(Y_ready, c * 12 + 2 * n + a + 1)
                        for h in range(4):
                            pe.matmul(bank4(a)[:, h, :], Tm[:, 4 * a + h, :], Yn[:, 4 * a + h, :],
                                      start=True, stop=True)
                        for h in range(4):
                            last = pe.matmul(bank4(2 + a)[:, h, :], Yn[:, 4 * a + h, :], Tm[:, 4 * a + h, :],
                                             start=True, stop=True)
                        last.then_inc(ZT_done, 1)
                for a in range(2):
                    pe.wait_ge(ZT_ready, c * 20 + 16 + 2 * a + 2)
                    for h in range(4):
                        last = pe.matmul(bank4(6 + a)[:, h, 64:P], L[64:P, 4 * a + h, :],
                                         Zm[64:P, 4 * a + h, 64:P], start=True, stop=True)
                    last.then_inc(Y_done, 1)
                for a in range(2):
                    pe.wait_ge(Y_ready, c * 12 + 10 + a + 1)
                    for h in range(4):
                        last = pe.matmul(bank4(a)[:, h, 64:P], Tm[0:64, 4 * a + h, :],
                                         Yn[0:64, 4 * a + h, 64:P], start=True, stop=True)
                    last.then_inc(ZT_done, 1)
                pe.wait_ge(qkT_ready, c * 2 + 2)
                for a in range(2):
                    for h in range(4):
                        last = pe.matmul(bank4(4 + a)[:, h, :], kS[:, 4 * a + h, :], S[:, 4 * a + h, :],
                                         start=True, stop=True)
                    last.then_inc(ks_done, 1)
                for a in range(2):
                    for h in range(4):
                        last = pe.matmul(bank4(6 + a)[:, h, :], qS[:, 4 * a + h, :], S[:, 4 * a + h, :],
                                         start=True, stop=True)
                    last.then_inc(qs_done, 1)
                for a in range(2):
                    pe.wait_ge(X_ready, c * 8 + 4 * a + 4 + 1)
                    pe.wait_ge(Z_ready, c * 4 + 2 + a + 1)
                    for h in range(4):
                        last = pe.matmul(bank4(a)[:, h, :], Zm[:, 4 * a + h, :], X[:, 4 * a + h, :],
                                         start=True, stop=True)
                    last.then_inc(w_done, 1)
                for a in range(2):
                    pe.wait_ge(w_ready, c * 2 + a + 1)
                    for h in range(4):
                        last = pe.matmul(bank4(4 + a)[:, h, :], Kd[:, 4 * a + h, :], w[:, 4 * a + h, :],
                                         start=True, stop=True)
                    last.then_inc(S_done, 1)
                    for h in range(4):
                        last = pe.matmul(bank4(2 + a)[:, h, :], qkT[:, 4 * a + h, :], w[:, 4 * a + h, :],
                                         start=True, stop=True)
                    last.then_inc(qkw_done, 1)
                pe.wait_ge(of_ready, c + 1 + 1)
                for a in range(2):
                    for h in range(4):
                        last = turn(bank4(6 + a)[:, h, :], of[:, 4 * a + h, :])
                    last.then_inc(of_turned, 1)

            pe.wait_ge(S_ready, TT * H + 1)
            pe.wait_ge(oT_ready, 2 * TT + 1)
            with pe.Fori(0, H // 4) as i:
                for r in range(4):
                    pe.wait_ge(z_gate, i * 4 + 1)
                    unit(i + Z0, r, h_hi, h_lo)
            pe.wait_ge(a_low, H + 1)

            def merges(first, n, hi, lo, gate_sem, merge_sem, both=False):
                with pe.Fori(0, n) as i:
                    for r in range(4):
                        if r % 2:
                            pe.wait_ge(merge_sem, i * 2 + 1)
                            unit(i + first, r, hi, lo)
                        else:
                            pe.wait_ge(gate_sem, i * 2 + 1)
                            unit(i + first, r, h_hi, h_lo)

            merges(A0, KT // 2, a_hi, a_lo, ma_gate, a_merged)
            pe.wait_ge(a_merged, KT + 1)

            def fox(i, products, attention):
                a = i - 1

                def score(t):
                    h, b = TASKS[t]

                    def go():
                        if t == 0:
                            pe.wait_ge(b_mul, a + 1)
                            pe.wait_ge(q_taken, 2 * a + 2)
                            pe.wait_ge(k_taken, 2 * a + 2)
                        if t == 1:
                            pe.wait_ge(v_ready, a + 1)
                        if t == 2:
                            pe.wait_ge(probsT_ready, 8 * a + 1)
                        if t >= 3:
                            pe.wait_ge(score_taken, 8 * a + t - 2)
                        n = (b + 1) * P
                        pe.matmul(ps[:, 4 + t % 3, 0:n], qx[:, h, b * P:n], kx[:, h, 0:n], start=True, stop=False)
                        pe.matmul(ps[:, 4 + t % 3, b * P:n], ident_b[:, :], mask_b[:, :], start=False,
                                  stop=True).then_inc(score_done, 1)
                    return go

                def probs_turn(t):
                    h, b = TASKS[t]

                    def go():
                        pe.wait_ge(probs_ready, 8 * a + t + 1)
                        if t == 0:
                            pe.wait_ge(score_taken, 8 * a + 8)
                        if t >= 3:
                            pe.wait_ge(probsT_ready, 8 * a + t - 2 + 1)
                        for k in range(b + 1):
                            s = START[t] + k * P
                            last = turn(ps[:, 4 + t % 3, k * P:(k + 1) * P], probs[:, s:s + P])
                        last.then_inc(probs_turned, 1)
                    return go

                def values(t):
                    h, b = TASKS[t]

                    def go():
                        pe.wait_ge(probsT_ready, 8 * a + t + 1 + 1)
                        if t == 0:
                            pe.wait_ge(o_taken, 2 * a + 1)
                        for k in range(b + 1):
                            s = START[t] + k * P
                            last = pe.matmul(ps[:, 7, t * FD:(t + 1) * FD], probsT[:, s:s + P],
                                             v_nat[:, k, h * FD:(h + 1) * FD], start=(k == 0), stop=(k == b))
                        if t == 7:
                            last.then_inc(pv_done, 1)
                    return go

                def o_turn():
                    pe.wait_ge(o_taken, 2 * a + 2 + 1)
                    for b in range(TT):
                        last = turn(ps[:, 4, b * P:(b + 1) * P], o_nat[:, b, :])
                    last.then_inc(o_turned, 1)

                def v_turn():
                    pe.wait_ge(v_taken, i + 1)
                    for b in range(TT):
                        last = turn(ps[:, 5, b * P:(b + 1) * P], vT[:, b * P:(b + 1) * P])
                    last.then_inc(v_back, 1)

                if products:
                    q = i + FOX0
                    both = range(8) if attention else ()
                    if attention:
                        pe.wait_ge(v_taken, i)
                    unit(q, 0, h_hi, h_lo, [score(t) for t in both])
                    if attention:
                        pe.wait_ge(q_taken, 2 * i)
                    unit(q, 1, h_hi, h_lo, [probs_turn(t) for t in both])
                    if attention:
                        pe.wait_ge(k_taken, 2 * i)
                    unit(q, 2, h_hi, h_lo, [values(t) for t in both])
                    if attention:
                        pe.wait_ge(fo_exp, i)
                    unit(q, 3, h_hi, h_lo, [o_turn, v_turn] if attention else [v_turn])
                else:
                    for t in range(8):
                        score(t)()
                    for t in range(8):
                        probs_turn(t)()
                    for t in range(8):
                        values(t)()
                    o_turn()

            fox(0, True, False)
            with pe.Fori(1, FH // 2) as i:
                fox(i, True, True)
            fox(FH // 2, False, True)

            pe.wait_ge(b_low, FH // 2 + 1)
            merges(B0, KT // 2, b_hi, b_lo, mb_gate, b_gated)

            pe.wait_ge(y_low, KT + 1)
            with pe.Fori(0, KT // 4) as i:
                def back_turn(r):
                    def go():
                        pe.wait_ge(out_taken, i * 4 + r + 1)
                        if r < 2:
                            pe.wait_ge(out_added, i * 4 + 1)
                        else:
                            pe.wait_ge(out_added, i * 4 + r - 1 + 1)
                        for t in range(TT):
                            last = turn(ps[:, 4 + r % 2, t * P:(t + 1) * P], back[:, r % 2, t * P:(t + 1) * P])
                        last.then_inc(out_turned, 1)
                    return go

                for r in range(4):
                    unit(i + OUT0, r, a_hi, a_lo, [back_turn(r - 1)] if r else [])
                back_turn(3)()

            turn_rows(1, xn2)
            pe.wait_ge(h_low, 2 * KT)
            merges(FFN0, FT // 2, h_hi, h_lo, ffn_gate, ffn_mul)

            pe.wait_ge(ffn_low, FT + 1)

            def down(q, r, k, first=False, final=False):
                pe.wait_ge(w_low, 4 * q + r + 1)
                n = 0
                for wt, xt in ((w_hi, f_hi), (w_hi, f_lo), (w_lo, f_hi)):
                    for kk in range(2):
                        for j in range(4):
                            s = kk * 512 + j * P
                            last = pe.matmul(ps[:, r % 2 * 4 + j, :], wt[:, r % 2, s:s + P],
                                             xt[:, bass.ds(k + kk, 1), :], start=(first and n < 4),
                                             stop=(final and n >= 20))
                            n += 1
                last.then_inc(unit_done, 1)

            for r in range(4):
                down(DOWN0, r, r // 2 * 2, first=(r < 2))
            with pe.Fori(1, FT // 4) as i:
                for r in range(4):
                    down(i + DOWN0, r, i * 4 + r // 2 * 2)
            for r in range(2):
                down(DOWN0 + FT // 4, r, FT - 2, final=True)
            for j in range(KT):
                pe.wait_ge(down_taken, j + 1)
                for t in range(TT):
                    last = turn(ps[:, j, t * P:(t + 1) * P], back[:, j % 2, t * P:(t + 1) * P])
                last.then_inc(down_turned, 1)


_INS = ["x", "norm_mix_w", "w_in", "conv_w", "a_log", "dt_bias", "gdn_norm_w", "fox_f_bias", "w_branch_a",
        "w_branch_b", "w_out", "norm_ffn_w", "w_gate", "w_up", "w_down", "norm_final_w"]


def kernel(**inputs):
    import numpy as _np
    import concourse.bacc as _bacc
    from concourse import mybir as _mybir
    from concourse.bass_utils import run_bass_kernel_spmd as _run

    nc = _bacc.Bacc("TRN2", target_bir_lowering=False, num_devices=1)
    arrays, args = {}, []
    for name in _INS:
        a = _np.ascontiguousarray(inputs[name])
        arrays[f"in_{name}"] = a
        args.append(nc.dram_tensor(f"in_{name}", a.shape, _mybir.dt.from_np(a.dtype), kind="ExternalInput").ap())
    shape = arrays["in_x"].shape
    args.append(nc.dram_tensor("out_0", shape, _mybir.dt.float32, kind="ExternalOutput").ap())
    hybrid_block(nc, *args)
    r = _run(nc, [arrays], core_ids=[0])
    return r.results[0]["out_0"]
```

```python
from contextlib import ExitStack

import concourse.bass as bass
from concourse import mybir

ALU = mybir.AluOpType
ACT = mybir.ActivationFunctionType
F32 = mybir.dt.float32
F32R = mybir.dt.float32r
BF16 = mybir.dt.bfloat16

P = 128
EPS = 1e-6
NEG = -1e30


def hybrid_block(nc, x, norm_mix_w, w_in, conv_w, a_log, dt_bias, gdn_norm_w, fox_f_bias, w_branch_a,
                 w_branch_b, w_out, norm_ffn_w, w_gate, w_up, w_down, norm_final_w, out):
    _, T, D = x.shape
    DK = gdn_norm_w.shape[1]
    H = a_log.shape[1]
    FH = fox_f_bias.shape[1]
    FD = D // FH
    TAPS = conv_w.shape[1]
    F = w_gate.shape[2]
    C = P
    TT, KT, FT = T // P, D // P, F // P
    NCONV = 3 * H
    assert (T, KT, DK, H, FH, FD, TAPS) == (512, 8, P, 8, 16, 64, 4) and FT % 2 == 0
    W = H * DK
    GZ, GA = 3 * W, 4 * W
    FQ = GA + 2 * H
    FK, FV, FF = FQ + D, FQ + 2 * D, FQ + 3 * D
    FO = FF + FH
    MA, MB = FO + D, FO + 2 * D
    UNIT = KT * P

    QKV0 = 0
    GATE0 = QKV0 + NCONV // 4
    FOX0 = GATE0 + 3 * KT // 4
    AB0 = FOX0 + FH // 2
    OUT0 = AB0 + 2 * KT // 4
    FFN0 = OUT0 + KT // 4
    DOWN0 = FFN0 + 2 * FT // 4

    NMIX, NFFN, GNW = TAPS * NCONV, TAPS * NCONV + KT, TAPS * NCONV + 2 * KT
    NPRM = GNW + 1

    cum_dram = nc.dram_tensor("cum_dram", [FH, T], F32).ap()
    gate_dram = nc.dram_tensor("gate_dram", [3, KT, P, T], F32).ap()
    GATES = (GZ, MA, MB)
    FILL = 6

    with ExitStack() as ctx:
        def sem(name):
            return ctx.enter_context(nc.semaphore(name))

        def keep(name, shape, dt=F32):
            return ctx.enter_context(nc.sbuf_tensor(name, shape, dt))

        h_hi = keep("h_hi", [P, KT, T], F32R)
        h_lo = keep("h_lo", [P, KT, T], F32R)
        raw = keep("raw", [P, 4, UNIT])
        w_hi = keep("w_hi", [P, 2, UNIT], F32R)
        w_lo = keep("w_lo", [P, 2, UNIT], F32R)
        mixT = keep("mixT", [P, KT, T])
        ident = keep("ident", [P, P])
        step = keep("step", [P, 7 * P])
        after = keep("after", [P, P])
        low = keep("low", [P, P])
        pair_neg = keep("pair_neg", [P, P])
        blk_neg = keep("blk_neg", [P, 5, P // 2])
        ident_b = keep("ident_b", [P, P], BF16)
        mask_b = keep("mask_b", [P, P], BF16)
        half_neg = keep("half_neg", [P, 2 * H])
        prm = keep("prm", [P, NPRM])
        gate = keep("gate", [P, 2, T])
        tmp = keep("tmp", [P, 2, T])
        ss = keep("ss", [P, 2 * TT])
        ms_half = keep("ms_half", [P, TT])
        ms = keep("ms", [P, TT])
        rstd = keep("rstd", [P, TT])

        with ExitStack() as part:
            def sb(name, shape, dt=F32):
                return part.enter_context(nc.sbuf_tensor(name, shape, dt))

            x_nat = sb("x_nat", [P, TT, D])
            xn = sb("xn", [P, TT, D])
            prm_rows = sb("prm_rows", [P, P])
            wsm = sb("wsm", [P, KT, P])
            wsm_hi = sb("wsm_hi", [P, KT, P], F32R)
            wsm_lo = sb("wsm_lo", [P, KT, P], F32R)
        with ExitStack() as part:
            def sb(name, shape, dt=F32):
                return part.enter_context(nc.sbuf_tensor(name, shape, dt))

            qkv = sb("qkv", [P, NCONV, T])
            qS = sb("qS", [P, H, C])
            kS = sb("kS", [P, H, C])
            vS = sb("vS", [P, H, C])
            Tm = sb("Tm", [P, H, C])
            Zm = sb("Zm", [P, H, C])
            gm = sb("gm", [P, H, C])
            E = sb("E", [P, H, C])
            L = sb("L", [P, H, C])
            Yn = sb("Yn", [P, H, C // 2])
            junk = sb("junk", [P, H, C])
            Kd = sb("Kd", [P, H, C])
            Vb = sb("Vb", [P, H, C])
            qk = sb("qk", [P, H, C])
            qkT = sb("qkT", [P, H, C])
            S = sb("S", [P, H, DK])
            gv = sb("gv", [P, TT, 3 * H])
            gabs = sb("gabs", [P, TT, 3 * H])
            sp = sb("sp", [P, TT, 3 * H])
            gb = sb("gb", [P, TT, H])
            beta = sb("beta", [P, TT * H])
            g = sb("g", [P, TT * H])
            gexp = sb("gexp", [P, 3, TT * H])
            bias_dt = sb("bias_dt", [P, H])
            bias_ff = sb("bias_ff", [P, FH])
            alog = sb("alog", [P, H])
            cum = sb("cum", [FH, T])
            ksum = sb("ksum", [P, 2 * H])
            nsum = sb("nsum", [P, 2 * H])
            rn = sb("rn", [P, 2 * H])
            bn = sb("bn", [P, H])
            bn2 = sb("bn2", [P, H])
            c1 = sb("c1", [P, H])
            oss = sb("oss", [P, H])
            osc = sb("osc", [P, H])
            cv = tmp
            Eb, X = gm, gm
            smT = Kd[0:32, 0:4, :].rearrange("p a n -> p (a n)")
            w = E
            o = vS
            of = qk
        with ExitStack() as part:
            def sb(name, shape, dt=F32):
                return part.enter_context(nc.sbuf_tensor(name, shape, dt))

            vT = sb("vT", [P, T])
            v_nat = sb("v_nat", [P, TT, P])
            q2 = sb("q2", [P, 2, T], F32R)
            k2 = sb("k2", [P, 2, T], F32R)
            kl2 = sb("kl2", [P, 2, T], F32R)
            zt = sb("zt", [P, T])
            NS = TT * (TT + 1) // 2 * P
            probs = sb("probs", [P, 2 * NS])
            probsT = sb("probsT", [P, 2 * NS])
            cumb = sb("cumb", [P, 2, T])
            scratch = sb("scratch", [P, 2 * TT])
            nmax = sb("nmax", [P, 2 * TT])
            psum_p = sb("psum_p", [P, 2 * TT])
            rsum = sb("rsum", [P, 2 * TT])
            o_nat = sb("o_nat", [P, TT, P])
            efo = gate[:, 0, :]
            a_hi = sb("a_hi", [P, KT, T], F32R)
            a_lo = sb("a_lo", [P, KT, T], F32R)
            b_hi = sb("b_hi", [P, KT, T], F32R)
            b_lo = sb("b_lo", [P, KT, T], F32R)
        with ExitStack() as part:
            def sb(name, shape, dt=F32):
                return part.enter_context(nc.sbuf_tensor(name, shape, dt))

            y_hi = sb("y_hi", [P, KT, T], F32R)
            y_lo = sb("y_lo", [P, KT, T], F32R)
            gin = sb("gin", [P, 2, 2, T])
        with ExitStack() as part:
            def sb(name, shape, dt=F32):
                return part.enter_context(nc.sbuf_tensor(name, shape, dt))

            with ExitStack() as inner:
                xn2 = inner.enter_context(nc.sbuf_tensor("xn2", [P, TT, D], F32))
            f_hi = sb("f_hi", [P, FT, T], F32R)
            f_lo = sb("f_lo", [P, FT, T], F32R)
            wfin = sb("wfin", [P, D])
        x_res = mixT[:, :, :].rearrange("p (t a) n -> p t (a n)", t=TT)
        back = tmp

        ps = ctx.enter_context(nc.psum_tensor("ps", [P, 8, 512], F32))

        x_loaded = [sem(f"x_loaded{t}") for t in range(TT)]
        prm_loaded = sem("prm_loaded")
        small_loaded = sem("small_loaded")
        w_loaded = [sem(f"w_loaded{s}") for s in range(4)]
        w_high = sem("w_high")
        w_low = sem("w_low")
        unit_done = sem("unit_done")
        consts_ready = sem("consts_ready")
        prm_turned = sem("prm_turned")
        prm_ready = sem("prm_ready")
        sq_summed = sem("sq_summed")
        ms_ready = sem("ms_ready")
        ms_halved = sem("ms_halved")
        rstd_ready = sem("rstd_ready")
        x_scaled = sem("x_scaled")
        x_turned = sem("x_turned")
        h_high = sem("h_high")
        h_low = sem("h_low")
        wsm_zero = sem("wsm_zero")
        wsm_high = sem("wsm_high")
        wsm_ready = sem("wsm_ready")
        small_taken = sem("small_taken")
        gate_exp = sem("gate_exp")
        gate_step = sem("gate_step")
        gate_sums = sem("gate_sums")
        gexp_ready = sem("gexp_ready")
        cum_taken = sem("cum_taken")
        cum_stored = sem("cum_stored")
        conv_seed = sem("conv_seed")
        conv_tap = sem("conv_tap")
        conv_bank = sem("conv_bank")
        conv_out = sem("conv_out")
        state_zero = sem("state_zero")
        staged = sem("staged")
        staged_v = sem("staged_v")
        squared = sem("squared")
        q_turned = sem("q_turned")
        sums_taken = sem("sums_taken")
        rn_ready = sem("rn_ready")
        row_step = sem("row_step")
        gm_ready = sem("gm_ready")
        D_done = sem("D_done")
        E_exp = sem("E_exp")
        E_masked = sem("E_masked")
        Eb_ready = sem("Eb_ready")
        k_turned = sem("k_turned")
        v_turned = sem("v_turned")
        Kd_ready = sem("Kd_ready")
        Vb_ready = sem("Vb_ready")
        G_done = sem("G_done")
        qk_done = sem("qk_done")
        L_ready = sem("L_ready")
        qk_ready = sem("qk_ready")
        T_step = sem("T_step")
        Z_turned = sem("Z_turned")
        Z_ready = sem("Z_ready")
        qk_turned = sem("qk_turned")
        qkT_ready = sem("qkT_ready")
        Y_done = sem("Y_done")
        Y_ready = sem("Y_ready")
        Zd_done = sem("Zd_done")
        Zd_added = sem("Zd_added")
        T_turned = sem("T_turned")
        T_ready = sem("T_ready")
        ks_done = sem("ks_done")
        qs_done = sem("qs_done")
        X_ready = sem("X_ready")
        qs_ready = sem("qs_ready")
        w_done = sem("w_done")
        w_ready = sem("w_ready")
        qkw_done = sem("qkw_done")
        S_done = sem("S_done")
        o_ready = sem("o_ready")
        S_ready = sem("S_ready")
        o_squared = sem("o_squared")
        osc_step = sem("osc_step")
        osc_pow = sem("osc_pow")
        of_ready = sem("of_ready")
        of_turned = sem("of_turned")
        oT_ready = sem("oT_ready")
        fill_taken = sem("fill_taken")
        gate_stored = [sem(f"gate_stored{s}") for s in range(2)]
        gin_loaded = [sem(f"gin_loaded{s}") for s in range(2)]
        small_unit = sem("small_unit")
        small_copied = sem("small_copied")
        small_back = sem("small_back")
        zt_loaded = sem("zt_loaded")
        z_mul = sem("z_mul")
        a_high = sem("a_high")
        a_low = sem("a_low")
        v_taken = sem("v_taken")
        q_taken = sem("q_taken")
        q_ready = sem("q_ready")
        k_taken = sem("k_taken")
        k_ready = sem("k_ready")
        fo_exp = sem("fo_exp")
        fo_step = sem("fo_step")
        cumb_loaded = sem("cumb_loaded")
        score_done = sem("score_done")
        score_taken = sem("score_taken")
        probs_ready = sem("probs_ready")
        probs_turned = sem("probs_turned")
        probsT_ready = sem("probsT_ready")
        rsum_ready = sem("rsum_ready")
        pv_done = sem("pv_done")
        o_taken = sem("o_taken")
        o_turned = sem("o_turned")
        v_back = sem("v_back")
        v_ready = sem("v_ready")
        b_mul = sem("b_mul")
        b_high = sem("b_high")
        b_low = sem("b_low")
        ab_gate = sem("ab_gate")
        ab_mul = sem("ab_mul")
        y_sum = sem("y_sum")
        y_high = sem("y_high")
        y_low = sem("y_low")
        xres_loaded = sem("xres_loaded")
        out_taken = sem("out_taken")
        out_turned = sem("out_turned")
        out_added = sem("out_added")
        ffn_gate = sem("ffn_gate")
        ffn_mul = sem("ffn_mul")
        ffn_high = sem("ffn_high")
        ffn_low = sem("ffn_low")
        wfin_loaded = sem("wfin_loaded")
        down_taken = sem("down_taken")
        down_turned = sem("down_turned")
        down_added = sem("down_added")
        fin_ready = sem("fin_ready")
        stored = sem("stored")

        LEAD = {conv_bank: 4, fill_taken: 2, gate_stored[0]: 16, gate_stored[1]: 16, ab_mul: 4, out_taken: 4,
                out_turned: 2, out_added: 2, ffn_gate: 2, ffn_mul: 2, ffn_low: 2, y_low: 2,
                y_sum: 2}
        for s in (a_low, b_low, b_mul, probsT_ready, o_taken, w_done, of_turned, of_ready, oT_ready, S_ready,
                  X_ready, o_ready):
            LEAD[s] = 1

        def led(s, n):
            return n + LEAD[s]

        block = ctx.enter_context(nc.Block())

        def heads(t):
            return t.unsqueeze(2).broadcast_to([P, t.shape[1], C])

        def half(t, q):
            return t[:, 4 * q:4 * q + 4, :]

        def banks(b, n=1):
            return ps[:, b:b + n, :]

        def half_bank(b):
            return ps[:, b, 0:256].rearrange("p (h c) -> p h c", h=4)

        def odd(t, n):
            if len(t.shape) == 3:
                return t.rearrange("p h (r two s) -> p h r two s", two=2, s=2 << n)[:, :, :, 1, :]
            return t.rearrange("p (r two s) -> p r two s", two=2, s=2 << n)[:, :, 1, :]

        def odd_like(t, n):
            return t.rearrange("p (r s) -> p r s", s=2 << n)

        def bank4(b):
            return ps[:, b, :].rearrange("p (h c) -> p h c", h=4)

        TASKS = [(h, b) for h in range(2) for b in range(TT)]
        START = [h * NS + b * (b + 1) // 2 * P for h, b in TASKS]

        @block.sync
        def _(sp):
            x_tiles = x[0].rearrange("(t p) d -> p t d", p=P)
            for t in range(TT):
                sp.dma_start(x_nat[:, t, :], x_tiles[:, t, :]).then_inc(x_loaded[t], 16)
            for row, src in ((0, conv_w[0].rearrange("w (n p) -> (w n) p", p=P)),
                             (NMIX, norm_mix_w[0].rearrange("(n p) -> n p", p=P)),
                             (NFFN, norm_ffn_w[0].rearrange("(n p) -> n p", p=P)), (GNW, gdn_norm_w)):
                sp.dma_start(prm_rows[row:row + src.shape[0], :], src).then_inc(prm_loaded, 16)

            def col_tile(wt, col):
                return wt[0].rearrange("(k p) n -> p k n", p=P)[:, :, bass.ds(col, P)]

            def load(q, r, src, first=False):
                if not first:
                    sp.wait_ge(w_low, 4 * q + r - 3)
                sp.dma_start(raw[:, r, :].rearrange("p (k n) -> p k n", n=src.shape[2]), src)\
                    .then_inc(w_loaded[r], 16)

            load(0, 0, col_tile(w_in, 0), True)
            for s, n in LEAD.items():
                sp.sem_inc(s, n)
            w_cols = w_in[0].rearrange("(k p) n -> p k n", p=P)
            sp.dma_start(wsm[:, :, 0:2 * H], w_cols[:, :, GA:GA + 2 * H]).then_inc(small_loaded, 16)
            sp.dma_start(wsm[:, :, 2 * H:32], w_cols[:, :, FF:FF + FH]).then_inc(small_loaded, 16)
            for r in range(1, 4):
                load(0, r, col_tile(w_in, r * P), True)
            sp.dma_start(bias_dt[:, :], dt_bias[0].partition_broadcast(P)).then_inc(small_loaded, 16)
            sp.dma_start(bias_ff[:, :], fox_f_bias[0].partition_broadcast(P)).then_inc(small_loaded, 16)
            sp.dma_start(alog[:, :], a_log[0].partition_broadcast(P)).then_inc(small_loaded, 16)
            with sp.Fori(1, NCONV // 4) as i:
                for r in range(4):
                    load(i, r, col_tile(w_in, i * (4 * P) + r * P))
            with sp.Fori(0, TT // 2) as i:
                for n in range(2 * FILL):
                    c2, u = divmod(n, FILL)
                    load(i * 3 + (GATE0 + n // 4), n % 4,
                         col_tile(w_in, i * (4 * P) + (GATES[u // 2] + (2 * c2 + u % 2) * P)))
            with sp.Fori(0, FH // 2) as i:
                for r, col in enumerate((FV, FQ, FK, FO)):
                    load(i + FOX0, r, col_tile(w_in, i * P + col))
            for s in range(2):
                sp.wait_ge(gate_stored[s], 16 * (3 * KT // 2) + LEAD[gate_stored[s]])
            with sp.Fori(0, KT // 2) as i:
                for r in range(4):
                    load(i + AB0, r, col_tile(w_branch_b if r >= 2 else w_branch_a,
                                              (i + AB0) * (2 * P) + (r % 2 - 2 * AB0) * P))
                for r in range(2):
                    sp.wait_ge(b_low, led(b_low, FH // 2))
                    sp.wait_ge(y_sum, led(y_sum, i * 2 + r - 1))
                    sp.dma_start(gin[:, r, :, :], gate_dram[1:3, bass.ds(i * 2 + r, 1)]
                                 .rearrange("k j p n -> p (k j) n")).then_inc(gin_loaded[r], 16)
            with sp.Fori(0, KT // 4) as i:
                for r in range(4):
                    load(i + OUT0, r, col_tile(w_out, i * (4 * P) + r * P))
            with sp.Fori(0, FT // 2) as i:
                for r in range(4):
                    load(i + FFN0, r, col_tile(w_up if r % 2 else w_gate, i * (2 * P) + r // 2 * P))
            down = w_down[0].rearrange("(k p) n -> p k n", p=P)
            sp.wait_ge(out_turned, led(out_turned, KT))
            sp.dma_start(wfin[:, :], norm_final_w.partition_broadcast(P)).then_inc(wfin_loaded, 16)
            with sp.Fori(0, FT // 4) as i:
                for r in range(4):
                    load(i + DOWN0, r, down[:, bass.ds(i * 4 + r // 2 * 2, 2), r % 2 * 512:r % 2 * 512 + 512])
            for r in range(2):
                load(DOWN0 + FT // 4, r, down[:, FT - 2:FT, r * 512:r * 512 + 512])
            y_tiles = out[0].rearrange("(t p) d -> p t d", p=P)
            for t in range(TT):
                sp.wait_ge(fin_ready, t + 1)
                sp.dma_start(y_tiles[:, t, :], x_res[:, t, :]).then_inc(stored, 16)
            sp.wait_ge(stored, 16 * TT)

        @block.gpsimd
        def _(pool):
            pool.memset(ident[:, :], 0.0).then_inc(consts_ready, 1)
            pool.memset(step[:, :], 1.0).then_inc(consts_ready, 1)
            pool.memset(after[:, :], 1.0).then_inc(consts_ready, 1)
            pool.memset(low[:, :], 1.0).then_inc(consts_ready, 1)
            pool.memset(pair_neg[:, :], 0.0).then_inc(consts_ready, 1)
            pool.memset(blk_neg[:, :, :], -1.0).then_inc(consts_ready, 1)
            pool.memset(ident_b[:, :], 0.0).then_inc(consts_ready, 1)
            pool.memset(mask_b[:, :], 0.0).then_inc(consts_ready, 1)
            pool.memset(half_neg[:, :], -0.5).then_inc(consts_ready, 1)
            pool.memset(wsm[:, :, 32:P], 0.0).then_inc(wsm_zero, 1)
            pool.wait_ge(consts_ready, 9)

            def select(t, pattern, base, cm, op, fill):
                return pool.affine_select(out=t, in_=t, compare_op=op, fill=fill, base=base, pattern=pattern,
                                          channel_multiplier=cm)

            select(ident[:, :], [[-1, P]], 0, 1, ALU.not_equal, 1.0).then_inc(consts_ready, 1)
            select(step[:, :], [[1, 7 * P]], -3 * P, -1, ALU.is_ge, 0.0).then_inc(consts_ready, 1)
            select(after[:, :], [[-1, P]], 0, 1, ALU.is_gt, 0.0).then_inc(consts_ready, 1)
            select(low[:, :], [[-1, P]], 0, 1, ALU.is_ge, 0.0).then_inc(consts_ready, 1)
            select(pair_neg[:, :].rearrange("p (r two) -> p r two", two=2)[:, :, 0],
                   [[-2, P // 2]], -1, 1, ALU.not_equal, -1.0).then_inc(consts_ready, 1)
            select(ident_b[:, :], [[-1, P]], 0, 1, ALU.not_equal, 1.0).then_inc(consts_ready, 1)
            select(mask_b[:, :], [[-1, P]], 0, 1, ALU.is_ge, NEG).then_inc(consts_ready, 1)
            for n in range(5):
                s = 2 << n
                v = blk_neg[:, n, :].rearrange("p (r s) -> p r s", s=s)
                select(v, [[-2 * s, P // (2 * s)], [0, s]], 0, 1, ALU.is_ge, 0.0).then_inc(consts_ready, 1)
                pool.wait_ge(consts_ready, 17 + 2 * n)
                select(v, [[2 * s, P // (2 * s)], [0, s]], s - 1, -1, ALU.is_ge, 0.0).then_inc(consts_ready, 1)

            def power(dst, src, n):
                return pool.tensor_tensor(dst, src, half_neg[:, 0:n], ALU.pow)

            def low_part(q, r):
                pool.wait_ge(w_high, 4 * q + r + 1)
                pool.tensor_tensor(w_lo[:, r % 2, :], raw[:, r, :], w_hi[:, r % 2, :], ALU.subtract)\
                    .then_inc(w_low, 1)

            def units(first, n):
                with pool.Fori(0, n) as i:
                    for r in range(4):
                        low_part(i + first, r)

            def row_norms(n):
                for t in range(TT):
                    pool.wait_ge(ms_ready, TT * n + t + 1)
                    power(rstd[:, t:t + 1], ms[:, t:t + 1], 1).then_inc(rstd_ready, 1)

            row_norms(0)
            units(QKV0, NCONV // 4)
            low_part(GATE0, 0)
            low_part(GATE0, 1)
            with pool.Fori(0, TT // 2) as i:
                for c2 in range(2):
                    c = i * 2 + c2

                    def ahead(u):
                        n = c2 * FILL + u + 2
                        low_part(i * 3 + (GATE0 + n // 4), n % 4)

                    pool.wait_ge(w_done, led(w_done, c * 2))
                    pool.tensor_tensor(gm[:, :, :], after[:, :].unsqueeze(1).broadcast_to([P, H, C]),
                                       heads(g[:, bass.ds(c * H, H)]), ALU.mult).then_inc(gm_ready, 1)
                    pool.wait_ge(sums_taken, c + 1)
                    power(rn[:, :], nsum[:, :], 2 * H).then_inc(rn_ready, 1)
                    ahead(0)
                    pool.wait_ge(E_masked, c + 1)
                    pool.wait_ge(row_step, c * 3 + 2)
                    pool.tensor_tensor(Eb[:, :, :], E[:, :, :], heads(bn2[:, :]), ALU.mult).then_inc(Eb_ready, 1)
                    ahead(1)
                    ahead(2)
                    ahead(3)
                    pool.wait_ge(osc_step, c * 4 + 3)
                    power(osc[:, :], oss[:, :], H).then_inc(osc_pow, 1)
                    ahead(4)
                    ahead(5)
            low_part(FOX0, 2)
            low_part(FOX0, 3)
            units(FOX0 + 1, FFN0 - FOX0 - 1)
            row_norms(1)
            units(FFN0, DOWN0 + FT // 4 - FFN0)
            for r in range(2):
                low_part(DOWN0 + FT // 4, r)
            row_norms(2)

        @block.scalar
        def _(act):
            def high_part(q, r, first=False):
                act.wait_ge(w_loaded[r], 16 * q + 16)
                if not first:
                    act.wait_ge(unit_done, 4 * q + r - 1)
                act.activation(w_hi[:, r % 2, :], raw[:, r, :], ACT.Copy).then_inc(w_high, 1)

            def high_ahead(q, r):
                high_part(q if r < 2 else q + 1, (r + 2) % 4)

            def half_squares(a, src, dst):
                cols = slice(a * D // 2, (a + 1) * D // 2)
                for t in range(TT):
                    act.activation(dst(t), src[:, t, cols], ACT.Square,
                                   accum_out=ss[:, a * TT + t:a * TT + t + 1]).then_inc(sq_summed, 1)

            def norm_high(n, col):
                for k in range(KT):
                    act.wait_ge(x_turned, KT * n + k + 1)
                    act.activation(h_hi[:, k, :], ps[:, k % 4, :], ACT.Copy,
                                   scale=prm[:, col + k:col + k + 1]).then_inc(h_high, 1)

            for t in range(TT):
                act.wait_ge(x_loaded[t], 16)
                act.activation(xn[:, t, :], x_nat[:, t, :], ACT.Square,
                               accum_out=ss[:, t:t + 1]).then_inc(sq_summed, 1)
            act.wait_ge(prm_turned, 1)
            act.activation(prm[:, :], ps[:, 7, 0:NPRM], ACT.Copy).then_inc(prm_ready, 1)
            high_part(0, 0, True)
            high_part(0, 1, True)
            act.wait_ge(prm_ready, 1)
            norm_high(0, NMIX)

            def conv(q, r, first=False):
                high_ahead(q, r)
                act.wait_ge(unit_done, 4 * q + r + 1)
                if not (first and r < 2):
                    act.wait_ge(conv_out, 4 * q + r - 1)
                act.activation(cv[:, r % 2, :], ps[:, r, :], ACT.Copy,
                               scale=prm[:, bass.ds(4 * q + (3 * NCONV + r), 1)]).then_inc(conv_seed, 1)
                act.wait_ge(conv_tap, 12 * q + 3 * r + 3)
                act.activation(qkv[:, bass.ds(4 * q + r, 1), :], cv[:, r % 2:r % 2 + 1, :], ACT.Silu)\
                    .then_inc(conv_out, 1)

            for r in range(4):
                conv(0, r, True)
            act.wait_ge(small_unit, 1)
            act.activation(smT, ps[0:32, 4, :], ACT.Copy).then_inc(small_copied, 1)
            for r in range(4):
                conv(1, r)
                if r == 1:
                    act.wait_ge(small_taken, 3)
                    act.activation(gabs[:, :, :], gv[:, :, :], ACT.Abs).then_inc(gate_exp, 1)
                    act.wait_ge(gate_exp, 1)
                    act.activation(gabs[:, :, :], gabs[:, :, :], ACT.Exp, scale=-1.0).then_inc(gate_exp, 1)
                    act.activation(gb[:, :, :], gb[:, :, :], ACT.Exp, scale=-1.0).then_inc(gate_exp, 1)
                    act.activation(alog[:, :], alog[:, :], ACT.Exp).then_inc(gate_exp, 1)
                    act.wait_ge(gate_exp, 2)
                    act.activation(gabs[:, :, :], gabs[:, :, :], ACT.Ln, bias=1.0).then_inc(gate_exp, 1)
            act.wait_ge(gate_sums, 2)
            act.activation(cum[:, :], ps[0:FH, 6, :], ACT.Copy).then_inc(cum_taken, 1)
            act.wait_ge(cum_taken, 1)
            act.dma_start(cum_dram, cum[:, :]).then_inc(cum_stored, 16)
            with act.Fori(2, NCONV // 4) as i:
                for r in range(4):
                    conv(i, r)

            act.wait_ge(gate_sums, 2)
            act.activation(gexp[:, :, :], ps[:, 5, 0:3 * TT * H].rearrange("p (a n) -> p a n", a=3),
                           ACT.Exp).then_inc(gexp_ready, 1)
            act.wait_ge(conv_out, NCONV)

            def chunk(i, c2):
                c = i * 2 + c2
                cols = bass.ds(c * C, C)

                def fill_done(u):
                    n = c2 * FILL + u
                    q, r = i * 3 + (GATE0 + n // 4), n % 4
                    high_ahead(q, r)
                    act.wait_ge(unit_done, 4 * q + r + 1)
                    s = gate_stored[u % 2]
                    act.wait_ge(s, led(s, c * (16 * FILL // 2) + 16 * (u // 2)))
                    act.activation(gate[:, u % 2, :], ps[:, 6 + u % 2, :], ACT.Copy if u >= 2 else ACT.Silu)\
                        .then_inc(fill_taken, 1)
                    act.wait_ge(fill_taken, led(fill_taken, c * FILL + u + 1))
                    act.dma_start(gate_dram[u // 2, bass.ds(c * 2 + u % 2, 1)].rearrange("a p n -> p (a n)"),
                                  gate[:, u % 2, :]).then_inc(s, 16)

                act.wait_ge(of_turned, led(of_turned, c * 2))
                act.activation(kS[:, :, :], qkv[:, H:2 * H, cols], ACT.Copy).then_inc(staged, 1)
                act.activation(qS[:, :, :], qkv[:, 0:H, cols], ACT.Copy).then_inc(staged, 1)
                for h in range(H):
                    act.wait_ge(k_turned, c * 2 + h // 4 + 1)
                    act.activation(junk[:, h, :], bank4(2 + h // 4)[:, h % 4, :], ACT.Square,
                                   accum_out=ksum[:, H + h:H + h + 1]).then_inc(squared, 1)
                for h in range(H):
                    act.wait_ge(q_turned, c * 2 + h // 4 + 1)
                    act.activation(of[:, h, :], bank4(h // 4)[:, h % 4, :], ACT.Square,
                                   accum_out=ksum[:, h:h + 1]).then_inc(squared, 1)
                fill_done(0)
                act.wait_ge(D_done, c * 2 + 2)
                act.activation(E[:, :, :].rearrange("p h c -> p (h c)"),
                               banks(0, 2).rearrange("p b n -> p (b n)"), ACT.Exp).then_inc(E_exp, 1)
                fill_done(1)
                for a in range(2):
                    act.wait_ge(Z_turned, c * 2 + a + 1)
                    act.activation(half(Zm, a), bank4(4 + a), ACT.Copy).then_inc(Z_ready, 1)
                for a in range(2):
                    act.wait_ge(qk_turned, c * 2 + a + 1)
                    act.activation(half(qkT, a), bank4(a), ACT.Copy).then_inc(qkT_ready, 1)
                for n in range(5):
                    for a in range(2):
                        act.wait_ge(T_turned, c * 10 + 2 * n + a + 1)
                        act.activation(half(Tm, a), bank4(4 + a), ACT.Copy).then_inc(T_ready, 1)
                    if n == 2:
                        fill_done(2)
                for a in range(2):
                    act.wait_ge(Y_done, c * 12 + 10 + a + 1)
                    act.activation(half(Yn, a)[0:64], half_bank(2 + a)[0:64], ACT.Copy, scale=-1.0)\
                        .then_inc(Y_ready, 1)
                for a in range(2):
                    act.wait_ge(Zd_done, c * 12 + 10 + a + 1)
                    act.activation(half(Zm, a)[0:64, :, 64:P], half_bank(4 + a)[0:64], ACT.Copy)\
                        .then_inc(Z_ready, 1)
                for h in range(H):
                    act.wait_ge(qs_done, c * 2 + h // 4 + 1)
                    act.activation(o[:, h, :], bank4(4 + h // 4)[:, h % 4, :], ACT.Copy,
                                   scale=gexp[:, 0, bass.ds(c * H + h, 1)]).then_inc(qs_ready, 1)
                for a in range(2):
                    act.wait_ge(w_done, led(w_done, c * 2 + a + 1))
                    act.activation(half(w, a), bank4(2 + a), ACT.Copy).then_inc(w_ready, 1)
                fill_done(3)
                for h in range(H):
                    act.wait_ge(o_ready, led(o_ready, c * 2 + h // 4 + 1))
                    act.activation(of[:, h, :], o[:, h, :], ACT.Square,
                                   accum_out=oss[:, h:h + 1]).then_inc(o_squared, 1)
                fill_done(4)
                for a in range(2):
                    act.wait_ge(of_turned, led(of_turned, c * 2 + a + 1))
                    act.activation(mixT[:, 4 * a:4 * a + 4, cols], bank4(2 + a), ACT.Copy).then_inc(oT_ready, 1)
                fill_done(5)

            with act.Fori(0, TT // 2) as i:
                chunk(i, 0)
                chunk(i, 1)

            def fox(i, products, attention):
                q = i + FOX0
                if products:
                    if attention:
                        act.wait_ge(z_mul, i)
                    act.dma_start(zt[:, :], gate_dram[0, bass.ds(i, 1)].rearrange("a p n -> p (a n)"))\
                        .then_inc(zt_loaded, 16)
                if attention:
                    for t, (h, b) in enumerate(TASKS):
                        act.wait_ge(score_taken, 8 * i - 8 + t + 1)
                        s = probs[:, START[t]:START[t] + (b + 1) * P]
                        act.activation(s, s, ACT.Exp, bias=nmax[:, t:t + 1], scale=-1.0,
                                       accum_out=psum_p[:, t:t + 1]).then_inc(probs_ready, 1)
                if products:
                    act.dma_start(cumb[:, :, :], cum_dram[bass.ds(2 * i, 2), :].partition_broadcast(P))\
                        .then_inc(cumb_loaded, 16)
                    high_ahead(q, 0)
                    act.wait_ge(unit_done, 4 * q + 1)
                    act.activation(vT[:, :], ps[:, 0, :], ACT.Copy).then_inc(v_taken, 1)
                    high_ahead(q, 1)
                    act.wait_ge(unit_done, 4 * q + 2)
                    for h in range(2):
                        act.activation(q2[0:FD, h, :], ps[h * FD:(h + 1) * FD, 1, :], ACT.Copy,
                                       scale=FD ** -0.5).then_inc(q_taken, 1)
                    high_ahead(q, 2)
                    act.wait_ge(unit_done, 4 * q + 3)
                    for h in range(2):
                        for v in range(2):
                            act.activation(k2[v * FD:(v + 1) * FD, h, :], ps[h * FD:(h + 1) * FD, 2, :],
                                           ACT.Copy).then_inc(k_taken, 1)
                    high_ahead(q, 3)
                    act.wait_ge(unit_done, 4 * q + 4)
                    if attention:
                        act.wait_ge(b_mul, led(b_mul, i))
                    act.activation(efo, ps[:, 3, :], ACT.Exp, scale=-1.0).then_inc(fo_exp, 1)

            act.wait_ge(cum_stored, 16)
            for s in range(2):
                act.wait_ge(gate_stored[s], led(gate_stored[s], 16 * (3 * KT // 2)))
            fox(0, True, False)
            with act.Fori(1, FH // 2) as i:
                fox(i, True, True)
            fox(FH // 2, False, True)

            def branches(i):
                for r in range(4):
                    high_ahead(i + AB0, r)
                    if r == 1:
                        for j in range(2):
                            act.wait_ge(gin_loaded[j], 16 * i + 16)
                            act.activation(gin[:, j, :, :], gin[:, j, :, :], ACT.Sigmoid).then_inc(ab_gate, 1)

            branches(0)
            act.wait_ge(a_low, led(a_low, KT))
            for t in range(TT):
                act.dma_start(x_res[:, t, :], x[0].rearrange("(t p) d -> p t d", p=P)[:, t, :])\
                    .then_inc(xres_loaded, 16)
            with act.Fori(1, KT // 2) as i:
                branches(i)

            for i in range(KT // 4):
                for r in range(4):
                    high_ahead(i + OUT0, r)
                    act.wait_ge(unit_done, (i + OUT0) * 4 + r + 1)
                    act.wait_ge(out_turned, led(out_turned, i * 4 + r - 1))
                    act.activation(back[:, r % 2, :], ps[:, r, :], ACT.Copy).then_inc(out_taken, 1)
                    if (i, r) == (1, 1):
                        act.wait_ge(out_added, led(out_added, 4))
                        half_squares(0, x_res, lambda t: gin[:, t // 2, t % 2, :])

            act.wait_ge(out_added, led(out_added, KT))
            half_squares(1, x_res, lambda t: xn2[:, t, D // 2:])
            norm_high(1, NFFN)

            def ffn(i):
                for r in range(4):
                    high_ahead(i + FFN0, r)
                    if r % 2 == 0:
                        act.wait_ge(unit_done, (i + FFN0) * 4 + r + 1)
                        act.wait_ge(ffn_mul, led(ffn_mul, i * 2 + r // 2 - 1))
                        act.activation(gate[:, r // 2, :], ps[:, r, :], ACT.Silu).then_inc(ffn_gate, 1)

            ffn(0)
            with act.Fori(1, FT // 2) as i:
                ffn(i)

            with act.Fori(0, FT // 4) as i:
                for r in range(4):
                    high_ahead(i + DOWN0, r)
            for j in range(KT):
                act.wait_ge(unit_done, 4 * (DOWN0 + FT // 4) + j // 4 + 1)
                if j >= 2:
                    act.wait_ge(down_turned, j - 1)
                act.activation(back[:, j % 2, :], ps[:, j, :], ACT.Copy).then_inc(down_taken, 1)
                if j == KT - 1:
                    act.wait_ge(down_added, KT // 2)
                    half_squares(0, x_res, lambda t: raw[:, 2 + t // 2, t % 2 * 512:t % 2 * 512 + 512])
            act.wait_ge(down_added, KT)
            half_squares(1, x_res, lambda t: raw[:, t // 2, t % 2 * 512:t % 2 * 512 + 512])

        @block.vector
        def _(dve):
            def copy(dst, src):
                return dve.tensor_copy(dst, src)

            def split(hi, lo, src, high, low_, n):
                copy(hi, src).then_inc(high, 1)
                dve.wait_ge(high, n + 1)
                dve.tensor_tensor(lo, src, hi.bitcast(F32), ALU.subtract).then_inc(low_, 1)

            def rms(n, scale):
                if n > 0:
                    dve.wait_ge(sq_summed, (2 * n) * TT)
                    dve.tensor_scalar(ms_half[:, :], ss[:, 0:TT], 1.0 / D, EPS, ALU.mult, ALU.add)\
                        .then_inc(ms_halved, 1)
                    dve.wait_ge(ms_halved, n)
                for t in range(TT + 1):
                    if t < TT and n == 0:
                        dve.wait_ge(sq_summed, t + 1)
                        dve.tensor_scalar(ms[:, t:t + 1], ss[:, t:t + 1], 1.0 / D, EPS, ALU.mult, ALU.add)\
                            .then_inc(ms_ready, 1)
                    elif t < TT:
                        dve.wait_ge(sq_summed, 2 * n * TT + t + 1)
                        dve.scalar_tensor_tensor(out=ms[:, t:t + 1], in0=ss[:, TT + t:TT + t + 1],
                                                 scalar=1.0 / D, in1=ms_half[:, t:t + 1], op0=ALU.mult,
                                                 op1=ALU.add).then_inc(ms_ready, 1)
                    if t > 0:
                        dve.wait_ge(rstd_ready, TT * n + t)
                        scale(t - 1)

            def norm_low(n, col):
                for k in range(KT):
                    dve.wait_ge(h_high, KT * n + k + 1)
                    dve.scalar_tensor_tensor(out=h_lo[:, k, :], in0=ps[:, k % 4, :],
                                             scalar=prm[:, col + k:col + k + 1],
                                             in1=h_hi[:, k, :].bitcast(F32), op0=ALU.mult,
                                             op1=ALU.subtract).then_inc(h_low, 1)

            rms(0, lambda t: dve.tensor_scalar(xn[:, t, :], x_nat[:, t, :], rstd[:, t:t + 1], None, ALU.mult)
                .then_inc(x_scaled, 1))
            norm_low(0, NMIX)
            dve.wait_ge(small_loaded, 16 * 5)
            dve.wait_ge(wsm_zero, 1)
            copy(wsm_hi[:, :, :], wsm[:, :, :]).then_inc(wsm_high, 1)
            dve.wait_ge(wsm_high, 1)
            dve.tensor_tensor(wsm_lo[:, :, :], wsm[:, :, :], wsm_hi[:, :, :].bitcast(F32), ALU.subtract)\
                .then_inc(wsm_ready, 1)

            def conv(q, r):
                dve.wait_ge(conv_seed, q * 4 + r + 1)
                for n in range(1, TAPS):
                    if n > 1:
                        dve.wait_ge(conv_tap, q * 12 + 3 * r + n - 1)
                    dve.scalar_tensor_tensor(
                        out=cv[:, r % 2, n:T], in0=ps[:, r, 0:T - n],
                        scalar=prm[:, bass.ds(q * 4 + ((TAPS - 1 - n) * NCONV + r), 1)],
                        in1=cv[:, r % 2, n:T], op0=ALU.mult, op1=ALU.add).then_inc(conv_tap, 1)
                dve.wait_ge(conv_tap, q * 12 + 3 * r + 3)
                dve.sem_inc(conv_bank, 1)

            for r in range(4):
                conv(0, r)
            small = ps[:, 5, 0:TT * 32].rearrange("p (t n) -> p t n", t=TT)
            for r in range(4):
                conv(1, r)
                if r == 0:
                    dve.wait_ge(small_back, 1)
                    dve.tensor_tensor(gv[:, :, 0:H], small[:, :, 0:H],
                                      bias_dt[:, :].unsqueeze(1).broadcast_to([P, TT, H]), ALU.add)\
                        .then_inc(small_taken, 1)
                    dve.scalar_tensor_tensor(out=gv[:, :, H:3 * H], in0=small[:, :, 2 * H:32], scalar=-1.0,
                                             in1=bias_ff[:, :].unsqueeze(1).broadcast_to([P, TT, FH]),
                                             op0=ALU.mult, op1=ALU.subtract).then_inc(small_taken, 1)
                    copy(gb[:, :, :], small[:, :, H:2 * H]).then_inc(small_taken, 1)
                if r == 2:
                    dve.wait_ge(gate_exp, 5)
                    dve.scalar_tensor_tensor(out=sp[:, :, :], in0=gv[:, :, :], scalar=0.0, in1=gabs[:, :, :],
                                             op0=ALU.max, op1=ALU.add).then_inc(gate_step, 1)
                    dve.tensor_scalar(gb[:, :, :], gb[:, :, :], 1.0, None, ALU.add).then_inc(gate_step, 1)
                    dve.wait_ge(gate_step, 2)
                    dve.reciprocal(beta[:, :].rearrange("p (t h) -> p t h", t=TT), gb[:, :, :])\
                        .then_inc(gate_step, 1)
                    dve.scalar_tensor_tensor(out=g[:, :].rearrange("p (t h) -> p t h", t=TT),
                                             in0=sp[:, :, 0:H], scalar=-1.0,
                                             in1=alog[:, :].unsqueeze(1).broadcast_to([P, TT, H]),
                                             op0=ALU.mult, op1=ALU.mult).then_inc(gate_step, 1)
            with dve.Fori(2, NCONV // 4) as i:
                for r in range(4):
                    conv(i, r)

            dve.memset(S[:, :, :], 0.0).then_inc(state_zero, 1)
            dve.wait_ge(state_zero, 1)
            dve.wait_ge(gexp_ready, 1)
            dve.wait_ge(conv_out, NCONV)

            def chunk(i, c2):
                c = i * 2 + c2
                cols = bass.ds(c * C, C)
                hc = bass.ds(c * H, H)
                dve.wait_ge(of_ready, led(of_ready, c))
                copy(vS[:, :, :], qkv[:, 2 * H:3 * H, cols]).then_inc(staged_v, 1)
                for a in range(2):
                    dve.wait_ge(squared, c * 16 + 4 * a + 4)
                    dve.tensor_tensor(half(Kd, a), bank4(2 + a),
                                      heads(gexp[:, 1, bass.ds(c * H + 4 * a, 4)]), ALU.mult)\
                        .then_inc(Kd_ready, 1)
                dve.wait_ge(squared, c * 16 + 16)
                dve.tensor_scalar(nsum[:, :], ksum[:, :], EPS, None, ALU.add).then_inc(sums_taken, 1)
                dve.wait_ge(rn_ready, c + 1)
                dve.tensor_tensor(bn[:, :], beta[:, hc], rn[:, H:2 * H], ALU.mult).then_inc(row_step, 1)
                dve.wait_ge(row_step, c * 3 + 1)
                dve.tensor_tensor(bn2[:, :], bn[:, :], rn[:, H:2 * H], ALU.mult).then_inc(row_step, 1)
                dve.wait_ge(row_step, c * 3 + 2)
                dve.scalar_tensor_tensor(out=c1[:, :], in0=bn2[:, :], scalar=-1.0, in1=gexp[:, 0, hc],
                                         op0=ALU.mult, op1=ALU.mult).then_inc(row_step, 1)
                for a in range(2):
                    dve.wait_ge(v_turned, c * 2 + a + 1)
                    dve.tensor_tensor(half(Vb, a), bank4(4 + a), heads(bn[:, 4 * a:4 * a + 4]), ALU.mult)\
                        .then_inc(Vb_ready, 1)
                dve.wait_ge(E_exp, c + 1)
                dve.tensor_tensor(E[:, :, :], E[:, :, :], low[:, :].unsqueeze(1).broadcast_to([P, H, C]),
                                  ALU.mult).then_inc(E_masked, 1)
                dve.wait_ge(E_masked, c + 1)
                dve.wait_ge(Eb_ready, c + 1)
                for a in range(2):
                    dve.wait_ge(G_done, c * 2 + a + 1)
                    dve.tensor_tensor(half(L, a), bank4(a), half(Eb, a), ALU.mult).then_inc(L_ready, 1)
                    dve.wait_ge(L_ready, c * 2 + a + 1)
                    dve.tensor_tensor(half(Tm, a), half(L, a), pair_neg[:, :].unsqueeze(1)
                                      .broadcast_to([P, 4, C]), ALU.mult).then_inc(T_step, 1)
                    dve.wait_ge(T_step, c * 4 + 2 * a + 1)
                    dve.tensor_tensor(half(Tm, a), half(Tm, a), ident[:, :].unsqueeze(1)
                                      .broadcast_to([P, 4, C]), ALU.add).then_inc(T_step, 1)
                for a in range(2):
                    dve.wait_ge(qk_done, c * 2 + a + 1)
                    dve.tensor_tensor(half(qk, a), bank4(2 + a), half(E, a), ALU.mult).then_inc(qk_ready, 1)
                for n in range(5):
                    for a in range(2):
                        dve.wait_ge(Y_done, c * 12 + 2 * n + a + 1)
                        dve.tensor_tensor(half(Yn, a), half_bank(2 + a), blk_neg[:, n:n + 1, :]
                                          .broadcast_to([P, 4, C // 2]), ALU.mult).then_inc(Y_ready, 1)
                    for a in range(2):
                        dve.wait_ge(Zd_done, c * 12 + 2 * n + a + 1)
                        if n == 0:
                            dve.wait_ge(Z_ready, c * 4 + a + 1)
                        z = odd(half(Zm, a), n)
                        dve.tensor_tensor(z, z, half_bank(a).rearrange("p h (r s) -> p h r s", s=2 << n),
                                          ALU.add).then_inc(Zd_added, 1)
                dve.wait_ge(Vb_ready, c * 2 + 2)
                dve.wait_ge(row_step, c * 3 + 3)
                for h in range(H):
                    dve.wait_ge(ks_done, c * 2 + h // 4 + 1)
                    dve.scalar_tensor_tensor(out=X[:, h, :], in0=bank4(h // 4)[:, h % 4, :],
                                             scalar=c1[:, h:h + 1], in1=Vb[:, h, :], op0=ALU.mult,
                                             op1=ALU.add).then_inc(X_ready, 1)
                for a in range(2):
                    dve.wait_ge(qkw_done, c * 2 + a + 1)
                    dve.wait_ge(qs_ready, c * 8 + 4 * a + 4)
                    dve.tensor_tensor(half(o, a), half(o, a), bank4(a), ALU.add).then_inc(o_ready, 1)
                for h in range(H):
                    dve.wait_ge(S_done, c * 2 + h // 4 + 1)
                    dve.scalar_tensor_tensor(out=S[:, h, :], in0=S[:, h, :],
                                             scalar=gexp[:, 2, bass.ds(c * H + h, 1)],
                                             in1=bank4(4 + h // 4)[:, h % 4, :], op0=ALU.mult,
                                             op1=ALU.add).then_inc(S_ready, 1)
                dve.wait_ge(o_squared, c * 8 + 8)
                dve.tensor_tensor(oss[:, :], oss[:, :], rn[:, 0:H], ALU.mult).then_inc(osc_step, 1)
                dve.wait_ge(osc_step, c * 4 + 1)
                dve.tensor_tensor(oss[:, :], oss[:, :], rn[:, 0:H], ALU.mult).then_inc(osc_step, 1)
                dve.wait_ge(osc_step, c * 4 + 2)
                dve.tensor_scalar(oss[:, :], oss[:, :], 1.0 / (DK * DK), EPS, ALU.mult, ALU.add)\
                    .then_inc(osc_step, 1)
                dve.wait_ge(osc_pow, c + 1)
                dve.scalar_tensor_tensor(out=osc[:, :], in0=osc[:, :], scalar=DK ** -0.5, in1=rn[:, 0:H],
                                         op0=ALU.mult, op1=ALU.mult).then_inc(osc_step, 1)
                dve.wait_ge(osc_step, c * 4 + 4)
                dve.wait_ge(o_ready, led(o_ready, c * 2 + 2))
                dve.tensor_tensor(of[:, :, :], o[:, :, :], heads(osc[:, :]), ALU.mult).then_inc(of_ready, 1)

            with dve.Fori(0, TT // 2) as i:
                chunk(i, 0)
                chunk(i, 1)

            def fox(i, products, attention):
                if attention:
                    for t, (h, b) in enumerate(TASKS):
                        if t == 0:
                            dve.wait_ge(cumb_loaded, 16 * i)
                        dve.wait_ge(score_done, 8 * i - 8 + t + 1)
                        dve.memset(scratch[:, t:t + 1], 0.0)
                        n = (b + 1) * P
                        dve.tensor_tensor_reduce(probs[:, START[t]:START[t] + n], ps[:, 4 + t % 3, 0:n],
                                                 cumb[:, h, 0:n], -1.0, 3.0e38, ALU.add, ALU.min,
                                                 nmax[:, t:t + 1]).then_inc(score_taken, 1)
                    for t, (h, b) in enumerate(TASKS):
                        dve.wait_ge(probs_turned, 8 * i - 8 + t + 1)
                        n = (b + 1) * P
                        copy(probsT[:, START[t]:START[t] + n], ps[:, 4 + t % 3, 0:n]).then_inc(probsT_ready, 1)
                if attention:
                    dve.wait_ge(fo_exp, i)
                    dve.tensor_scalar(efo, efo, 1.0, None, ALU.add).then_inc(fo_step, 1)
                    dve.wait_ge(fo_step, 2 * i - 1)
                    dve.reciprocal(efo, efo).then_inc(fo_step, 1)
                    dve.wait_ge(probs_ready, 8 * i)
                    dve.reciprocal(rsum[:, :], psum_p[:, :]).then_inc(rsum_ready, 1)
                if products:
                    dve.wait_ge(q_taken, 2 * i + 2)
                    for h in range(2):
                        dve.scalar_tensor_tensor(out=q2[FD:P, h, :], in0=ps[h * FD:(h + 1) * FD, 1, :],
                                                 scalar=FD ** -0.5, in1=q2[0:FD, h, :].bitcast(F32),
                                                 op0=ALU.mult, op1=ALU.subtract).then_inc(q_ready, 1)
                    dve.wait_ge(zt_loaded, 16 * i + 16)
                    if attention:
                        dve.wait_ge(a_low, led(a_low, i))
                    dve.scalar_tensor_tensor(out=tmp[:, 1:2, :], in0=mixT[:, bass.ds(i, 1), :],
                                             scalar=prm[:, GNW:GNW + 1], in1=zt[:, :].unsqueeze(1),
                                             op0=ALU.mult, op1=ALU.mult).then_inc(z_mul, 1)
                    dve.wait_ge(z_mul, i + 1)
                    split(a_hi[:, bass.ds(i, 1), :], a_lo[:, bass.ds(i, 1), :], tmp[:, 1:2, :],
                          a_high, a_low, i)
                if attention:
                    dve.wait_ge(rsum_ready, i)
                    dve.wait_ge(pv_done, i)
                    for h in range(2):
                        dve.tensor_tensor(
                            o_nat[:, :, h * FD:(h + 1) * FD],
                            ps[:, 7, :].rearrange("p (h b d) -> p h b d", h=2, b=TT)[:, h],
                            rsum[:, h * TT:(h + 1) * TT].unsqueeze(2).broadcast_to([P, TT, FD]),
                            ALU.mult).then_inc(o_taken, 1)
                if products:
                    for h in range(2):
                        dve.wait_ge(k_taken, 4 * i + 2 * h + 2)
                        for v in range(2):
                            dve.tensor_tensor(kl2[v * FD:(v + 1) * FD, h, :], ps[h * FD:(h + 1) * FD, 2, :],
                                              k2[0:FD, h, :].bitcast(F32), ALU.subtract).then_inc(k_ready, 1)
                    dve.wait_ge(v_back, i + 1)
                    copy(v_nat[:, :, :], ps[:, 5, :].rearrange("p (t n) -> p t n", t=TT)).then_inc(v_ready, 1)
                if attention:
                    dve.wait_ge(o_turned, i)
                    dve.wait_ge(fo_step, 2 * i)
                    dve.wait_ge(b_low, led(b_low, i - 1))
                    dve.tensor_tensor(tmp[:, 0, :], ps[:, 7, :], efo, ALU.mult).then_inc(b_mul, 1)
                    dve.wait_ge(b_mul, led(b_mul, i))
                    split(b_hi[:, bass.ds(i - 1, 1), :], b_lo[:, bass.ds(i - 1, 1), :], tmp[:, 0:1, :],
                          b_high, b_low, i - 1)

            dve.wait_ge(oT_ready, led(oT_ready, 2 * TT))
            fox(0, True, False)
            with dve.Fori(1, FH // 2) as i:
                fox(i, True, True)
            fox(FH // 2, False, True)

            dve.wait_ge(b_low, led(b_low, FH // 2))
            dve.wait_ge(a_low, led(a_low, KT))
            with dve.Fori(0, KT // 2) as i:
                for r in range(4):
                    k, j = r // 2, i * 2 + r % 2
                    row = bass.ds(j, 1)
                    dve.wait_ge(ab_gate, j + 1)
                    dve.wait_ge(unit_done, (i + AB0) * 4 + r + 1)
                    dve.tensor_tensor(gin[:, r % 2, k, :], gin[:, r % 2, k, :], ps[:, r, :], ALU.mult)\
                        .then_inc(ab_mul, 1)
                    if k == 1:
                        dve.wait_ge(y_low, led(y_low, j - 1))
                        dve.wait_ge(ab_mul, led(ab_mul, i * 4 + r + 1))
                        dve.tensor_tensor(tmp[:, r % 2, :], gin[:, r % 2, 0, :], gin[:, r % 2, 1, :], ALU.add)\
                            .then_inc(y_sum, 1)
                        dve.wait_ge(y_sum, led(y_sum, j + 1))
                        split(y_hi[:, row, :], y_lo[:, row, :], tmp[:, r % 2:r % 2 + 1, :], y_high, y_low, j)

            dve.wait_ge(xres_loaded, 16 * TT)
            with dve.Fori(0, KT // 4) as i:
                for r in range(4):
                    cols = bass.ds(i * (4 * P) + r * P, P)
                    dve.wait_ge(out_turned, led(out_turned, i * 4 + r + 1))
                    dve.tensor_tensor(x_res[:, :, cols], x_res[:, :, cols],
                                      ps[:, 4 + r % 2, :].rearrange("p (t n) -> p t n", t=TT), ALU.add)\
                        .then_inc(out_added, 1)
            rms(1, lambda t: dve.tensor_scalar(xn2[:, t, :], x_res[:, t, :], rstd[:, t:t + 1], None, ALU.mult)
                .then_inc(x_scaled, 1))
            norm_low(1, NFFN)
            with dve.Fori(0, FT // 2) as i:
                for r in range(2):
                    j = i * 2 + r
                    row = bass.ds(j, 1)
                    dve.wait_ge(unit_done, (i + FFN0) * 4 + 2 * r + 2)
                    dve.wait_ge(ffn_gate, led(ffn_gate, j + 1))
                    dve.wait_ge(ffn_low, led(ffn_low, j - 1))
                    dve.tensor_tensor(tmp[:, r:r + 1, :], gate[:, r:r + 1, :], ps[:, 2 * r + 1:2 * r + 2, :],
                                      ALU.mult).then_inc(ffn_mul, 1)
                    dve.wait_ge(ffn_mul, led(ffn_mul, j + 1))
                    split(f_hi[:, row, :], f_lo[:, row, :], tmp[:, r:r + 1, :], ffn_high, ffn_low, j)

            for j in range(KT):
                dve.wait_ge(down_turned, j + 1)
                dve.tensor_tensor(x_res[:, :, j * P:(j + 1) * P], x_res[:, :, j * P:(j + 1) * P],
                                  ps[:, j, :].rearrange("p (t n) -> p t n", t=TT), ALU.add)\
                    .then_inc(down_added, 1)
            dve.wait_ge(wfin_loaded, 16)
            rms(2, lambda t: dve.scalar_tensor_tensor(
                out=x_res[:, t, :], in0=x_res[:, t, :], scalar=rstd[:, t:t + 1], in1=wfin[:, :], op0=ALU.mult,
                op1=ALU.mult).then_inc(fin_ready, 1))

        @block.tensor
        def _(pe):
            def turn(dst, src):
                return pe.transpose(dst, src, ident[:src.shape[0], :src.shape[0]])

            def turn_rows(n, src):
                for k in range(KT):
                    if k >= 4:
                        pe.wait_ge(h_low, KT * n + k - 3)
                    for t in range(TT):
                        if k == 0:
                            pe.wait_ge(x_scaled, TT * n + t + 1)
                        last = turn(ps[:, k % 4, t * P:(t + 1) * P], src[:, t, k * P:(k + 1) * P])
                    last.then_inc(x_turned, 1)

            PASSES = [(wl, xl, k) for k in range(KT) for wl, xl in ((0, 0), (0, 1), (1, 0))]

            def product(bank, wts, acts, n):
                wl, xl, k = PASSES[n]
                return pe.matmul(ps[:, bank, :], wts[wl][k], acts[xl][:, k, :], start=(n == 0),
                                 stop=(n == len(PASSES) - 1))

            def slot(r):
                return [[half_w[:, r % 2, k * P:(k + 1) * P] for k in range(KT)] for half_w in (w_hi, w_lo)]

            def unit(q, r, hi, lo, tasks=(), last_input=None):
                pe.wait_ge(w_low, 4 * q + r + 1)
                tasks = list(tasks)
                every = max(1, len(PASSES) // max(1, len(tasks)))
                for n in range(len(PASSES)):
                    if last_input and n == len(PASSES) - 3:
                        pe.wait_ge(*last_input)
                    if tasks and n % every == every - 1:
                        tasks.pop(0)()
                    last = product(r, slot(r), (hi, lo), n)
                last.then_inc(unit_done, 1)
                for task in tasks:
                    task()

            pe.wait_ge(consts_ready, 26)
            pe.wait_ge(prm_loaded, 64)
            turn(ps[:, 7, 0:NPRM], prm_rows[0:NPRM, :]).then_inc(prm_turned, 1)
            turn_rows(0, xn)

            def conv(q, r, last_input=None):
                pe.wait_ge(conv_bank, q * 4 + r + 1)
                unit(q, r, h_hi, h_lo, (), last_input)

            pe.wait_ge(h_low, KT - 1)
            for r in range(4):
                conv(0, r, None if r else (h_low, KT))
            pe.wait_ge(wsm_ready, 1)
            small_w = [[half_w[:, k, :] for k in range(KT)] for half_w in (wsm_hi, wsm_lo)]
            for n in range(len(PASSES)):
                last = product(4, small_w, (h_hi, h_lo), n)
            last.then_inc(small_unit, 1)
            for r in range(4):
                conv(1, r)
                if r == 0:
                    pe.wait_ge(small_copied, 1)
                    for t in range(TT):
                        last = turn(ps[:, 5, t * 32:(t + 1) * 32], smT[:, t * P:(t + 1) * P])
                    last.then_inc(small_back, 1)
            pe.wait_ge(gate_step, 4)
            for n, lhs in enumerate((step[:, 3 * P:4 * P], after[:, :], step[:, 4 * P:5 * P])):
                last = pe.matmul(ps[:, 5, n * TT * H:(n + 1) * TT * H], lhs, g[:, :], start=True, stop=True)
            last.then_inc(gate_sums, 1)
            for t in range(TT):
                last = pe.matmul(ps[0:FH, 6, :], sp[:, t, H:3 * H], step[:, (3 - t) * P:(3 - t) * P + T],
                                 start=(t == 0), stop=(t == TT - 1))
            last.then_inc(gate_sums, 1)
            with pe.Fori(2, NCONV // 4) as i:
                for r in range(4):
                    conv(i, r)

            pe.wait_ge(cum_taken, 1)

            def chunk(i, c2):
                c = i * 2 + c2
                at = [0]

                def fill(m):
                    for _ in range(m):
                        u, n = divmod(at[0], len(PASSES))
                        nn = c2 * FILL + u
                        q, r = i * 3 + (GATE0 + nn // 4), nn % 4
                        if n == 0:
                            pe.wait_ge(w_low, 4 * q + r + 1)
                            pe.wait_ge(fill_taken, led(fill_taken, c * FILL + u - 1))
                        last = product(6 + u % 2, slot(r), (h_hi, h_lo), n)
                        if n == len(PASSES) - 1:
                            last.then_inc(unit_done, 1)
                        at[0] += 1

                def per_head(a, do, sem_):
                    for h in range(4):
                        last = do(h, 4 * a + h)
                    last.then_inc(sem_, 1)

                def mm(dst, lhs, rhs):
                    return pe.matmul(dst, lhs, rhs, start=True, stop=True)

                fill(20)
                pe.wait_ge(conv_tap, 3 * NCONV)
                pe.wait_ge(gexp_ready, 1)
                pe.wait_ge(staged, c * 2 + 1)
                pe.wait_ge(oT_ready, led(oT_ready, c * 2))
                for a in range(2):
                    per_head(a, lambda h, n: turn(bank4(2 + a)[:, h, :], kS[:, n, :]), k_turned)
                pe.wait_ge(staged, c * 2 + 2)
                pe.wait_ge(o_ready, led(o_ready, c * 2))
                for a in range(2):
                    per_head(a, lambda h, n: turn(bank4(a)[:, h, :], qS[:, n, :]), q_turned)
                fill(2)
                pe.wait_ge(staged_v, c + 1)
                pe.wait_ge(S_ready, led(S_ready, c * 8))
                for a in range(2):
                    per_head(a, lambda h, n: turn(bank4(4 + a)[:, h, :], vS[:, n, :]), v_turned)
                fill(6)
                pe.wait_ge(squared, c * 16 + 16)
                pe.wait_ge(gm_ready, c + 1)
                for a in range(2):
                    mm(ps[:, a, :], step[:, 3 * P:4 * P], half(gm, a).rearrange("p h c -> p (h c)"))\
                        .then_inc(D_done, 1)
                fill(12)
                pe.wait_ge(E_exp, c + 1)
                for a in range(2):
                    per_head(a, lambda h, n: mm(bank4(a)[:, h, :], kS[:, n, :], kS[:, n, :]), G_done)
                fill(8)
                pe.wait_ge(Kd_ready, c * 2 + 2)
                for a in range(2):
                    per_head(a, lambda h, n: mm(bank4(2 + a)[:, h, :], qS[:, n, :], kS[:, n, :]), qk_done)
                fill(8)
                for a in range(2):
                    pe.wait_ge(T_step, c * 4 + 2 * a + 2)
                    pe.wait_ge(Vb_ready, c * 2 + a + 1)
                    per_head(a, lambda h, n: turn(bank4(4 + a)[:, h, :], Tm[:, n, :]), Z_turned)
                for a in range(2):
                    pe.wait_ge(qk_ready, c * 2 + a + 1)
                    per_head(a, lambda h, n: turn(bank4(a)[:, h, :], qk[:, n, :]), qk_turned)
                fill(4)
                for v in range(5):
                    for a in range(2):
                        if v == 0:
                            pe.wait_ge(Z_ready, c * 4 + a + 1)
                        else:
                            pe.wait_ge(Zd_added, c * 10 + 2 * v - 2 + a + 1)
                        per_head(a, lambda h, n: mm(odd_like(half_bank(2 + a)[:, h, :], v), L[:, n, :],
                                                    odd(Zm[:, n, :], v)), Y_done)
                    fill(2)
                    for a in range(2):
                        pe.wait_ge(Y_ready, c * 12 + 2 * v + a + 1)
                        if v > 0:
                            pe.wait_ge(T_ready, c * 10 + 2 * v - 2 + a + 1)
                        else:
                            pe.wait_ge(qkT_ready, c * 2 + a + 1)
                        per_head(a, lambda h, n: mm(half_bank(a)[:, h, :], Tm[:, n, :], Yn[:, n, :]), Zd_done)
                    fill(2)
                    for a in range(2):
                        pe.wait_ge(Zd_added, c * 10 + 2 * v + a + 1)
                        per_head(a, lambda h, n: turn(bank4(4 + a)[:, h, :], Zm[:, n, :]), T_turned)
                for a in range(2):
                    per_head(a, lambda h, n: mm(half_bank(2 + a)[:, h, :], L[64:P, n, :], Zm[64:P, n, 64:P]),
                             Y_done)
                fill(2)
                for a in range(2):
                    pe.wait_ge(T_ready, c * 10 + 8 + a + 1)
                    pe.wait_ge(Y_ready, c * 12 + 10 + a + 1)
                    per_head(a, lambda h, n: mm(half_bank(4 + a)[:, h, :], Tm[0:64, n, :], Yn[0:64, n, :]), Zd_done)
                fill(2)
                for a in range(2):
                    per_head(a, lambda h, n: mm(bank4(a)[:, h, :], kS[:, n, :], S[:, n, :]), ks_done)
                pe.wait_ge(Z_ready, c * 4 + 4)
                for a in range(2):
                    per_head(a, lambda h, n: mm(bank4(4 + a)[:, h, :], qS[:, n, :], S[:, n, :]), qs_done)
                fill(8)
                for a in range(2):
                    pe.wait_ge(X_ready, led(X_ready, c * 8 + 4 * a + 4))
                    per_head(a, lambda h, n: mm(bank4(2 + a)[:, h, :], Zm[:, n, :], X[:, n, :]), w_done)
                fill(10)
                for a in range(2):
                    pe.wait_ge(w_ready, c * 2 + a + 1)
                    per_head(a, lambda h, n: mm(bank4(a)[:, h, :], qkT[:, n, :], w[:, n, :]), qkw_done)
                for a in range(2):
                    pe.wait_ge(qs_ready, c * 8 + 4 * a + 4)
                    per_head(a, lambda h, n: mm(bank4(4 + a)[:, h, :], Kd[:, n, :], w[:, n, :]), S_done)
                fill(30)
                pe.wait_ge(of_ready, led(of_ready, c + 1))
                for a in range(2):
                    per_head(a, lambda h, n: turn(bank4(2 + a)[:, h, :], of[:, n, :]), of_turned)
                fill(FILL * len(PASSES) - at[0])

            with pe.Fori(0, TT // 2) as i:
                chunk(i, 0)
                chunk(i, 1)

            def fox(i, products, attention):
                a = i - 1

                def score(t):
                    h, b = TASKS[t]

                    def go():
                        if t == 0:
                            pe.wait_ge(q_ready, 2 * i)
                            pe.wait_ge(k_ready, 4 * i)
                        if t == 1:
                            pe.wait_ge(v_ready, i)
                        if t == 2:
                            pe.wait_ge(probsT_ready, led(probsT_ready, 8 * a))
                        if t >= 3:
                            pe.wait_ge(score_taken, 8 * a + t - 2)
                        n = (b + 1) * P
                        pe.matmul(ps[:, 4 + t % 3, 0:n], q2[:, h, b * P:n], k2[:, h, 0:n], start=True, stop=False)
                        pe.matmul(ps[:, 4 + t % 3, 0:n], q2[:, h, b * P:n], kl2[:, h, 0:n], start=False,
                                  stop=False)
                        pe.matmul(ps[:, 4 + t % 3, b * P:n], ident_b[:, :], mask_b[:, :], start=False,
                                  stop=True).then_inc(score_done, 1)
                    return go

                def probs_turn(t):
                    h, b = TASKS[t]

                    def go():
                        pe.wait_ge(probs_ready, 8 * a + t + 1)
                        if t == 0:
                            pe.wait_ge(score_taken, 8 * a + 8)
                        if t >= 3:
                            pe.wait_ge(probsT_ready, led(probsT_ready, 8 * a + t - 2))
                        for k in range(b + 1):
                            s = START[t] + k * P
                            last = turn(ps[:, 4 + t % 3, k * P:(k + 1) * P], probs[:, s:s + P])
                        last.then_inc(probs_turned, 1)
                    return go

                def values(t):
                    h, b = TASKS[t]

                    def go():
                        pe.wait_ge(probsT_ready, led(probsT_ready, 8 * a + t + 1))
                        if t == 0:
                            pe.wait_ge(b_mul, led(b_mul, a))
                        for k in range(b + 1):
                            s = START[t] + k * P
                            last = pe.matmul(ps[:, 7, t * FD:(t + 1) * FD], probsT[:, s:s + P],
                                             v_nat[:, k, h * FD:(h + 1) * FD], start=(k == 0), stop=(k == b))
                        if t == 7:
                            last.then_inc(pv_done, 1)
                    return go

                def o_turn():
                    pe.wait_ge(o_taken, led(o_taken, 2 * a + 2))
                    for b in range(TT):
                        last = turn(ps[:, 7, b * P:(b + 1) * P], o_nat[:, b, :])
                    last.then_inc(o_turned, 1)

                def v_turn():
                    pe.wait_ge(v_taken, i + 1)
                    for b in range(TT):
                        last = turn(ps[:, 5, b * P:(b + 1) * P], vT[:, b * P:(b + 1) * P])
                    last.then_inc(v_back, 1)

                if products:
                    q = i + FOX0
                    both = range(8) if attention else ()
                    if attention:
                        pe.wait_ge(v_taken, i)
                    unit(q, 0, h_hi, h_lo, [score(t) for t in both])
                    unit(q, 1, h_hi, h_lo, [probs_turn(t) for t in both])
                    unit(q, 2, h_hi, h_lo, [values(t) for t in both])
                    if attention:
                        pe.wait_ge(fo_exp, i)
                    unit(q, 3, h_hi, h_lo, [v_turn, o_turn] if attention else [v_turn])
                else:
                    for t in range(8):
                        score(t)()
                    pe.wait_ge(fo_exp, i)
                    pe.wait_ge(a_low, led(a_low, KT))
                    unit(AB0, 0, a_hi, a_lo, [probs_turn(t) for t in range(8)])
                    for t in range(8):
                        values(t)()
                    unit(AB0, 1, a_hi, a_lo)
                    o_turn()

            pe.wait_ge(fill_taken, led(fill_taken, FILL * TT))
            pe.wait_ge(oT_ready, led(oT_ready, 2 * TT))
            fox(0, True, False)
            with pe.Fori(1, FH // 2) as i:
                fox(i, True, True)
            fox(FH // 2, False, True)

            pe.wait_ge(b_low, led(b_low, FH // 2 - 1))
            for r in range(2, 4):
                unit(AB0, r, b_hi, b_lo, (), None if r > 2 else (b_low, led(b_low, FH // 2)))
            with pe.Fori(1, KT // 2) as i:
                for r in range(4):
                    pe.wait_ge(ab_mul, led(ab_mul, i * 4 + r - 3))
                    unit(i + AB0, r, b_hi if r >= 2 else a_hi, b_lo if r >= 2 else a_lo)

            def out_group(i):
                def back_turn(r):
                    def go():
                        pe.wait_ge(out_taken, led(out_taken, i * 4 + r + 1))
                        pe.wait_ge(out_added, led(out_added, i * 4 + r - 1))
                        for t in range(TT):
                            last = turn(ps[:, 4 + r % 2, t * P:(t + 1) * P], back[:, r % 2, t * P:(t + 1) * P])
                        last.then_inc(out_turned, 1)
                    return go

                for r in range(4):
                    pe.wait_ge(out_taken, led(out_taken, i * 4 + r - 3))
                    unit(i + OUT0, r, y_hi, y_lo, [back_turn(r - 1)] if i or r else [],
                         None if i or r else (y_low, led(y_low, KT)))
                if i == KT // 4 - 1:
                    back_turn(3)()

            pe.wait_ge(ab_mul, led(ab_mul, 2 * KT - 2))
            pe.wait_ge(y_low, led(y_low, KT - 1))
            out_group(0)
            out_group(1)

            turn_rows(1, xn2)

            def ffn(i, last_input=None):
                for r in range(4):
                    s = ffn_mul if r % 2 else ffn_gate
                    pe.wait_ge(s, led(s, i * 2 + r // 2 - 1))
                    unit(i + FFN0, r, h_hi, h_lo, (), None if r else last_input)

            pe.wait_ge(h_low, 2 * KT - 1)
            ffn(0, (h_low, 2 * KT))
            with pe.Fori(1, FT // 2) as i:
                ffn(i)

            def down_turn(j):
                pe.wait_ge(down_taken, j + 1)
                for t in range(TT):
                    last = turn(ps[:, j, t * P:(t + 1) * P], back[:, j % 2, t * P:(t + 1) * P])
                last.then_inc(down_turned, 1)

            def down(q, r, k, first=False, final=False):
                pe.wait_ge(w_low, 4 * q + r + 1)
                n = 0
                for wt, xt in ((w_hi, f_hi), (w_hi, f_lo), (w_lo, f_hi)):
                    for kk in range(2):
                        for j in range(4):
                            s = kk * 512 + j * P
                            last = pe.matmul(ps[:, r % 2 * 4 + j, :], wt[:, r % 2, s:s + P],
                                             xt[:, bass.ds(k + kk, 1), :], start=(first and n < 4),
                                             stop=(final and n >= 20))
                            n += 1
                            if final and r == 1 and n % 5 == 2 and n > 5:
                                down_turn(n // 5 - 1)
                last.then_inc(unit_done, 1)

            pe.wait_ge(ffn_mul, led(ffn_mul, FT))
            pe.wait_ge(ffn_low, led(ffn_low, FT - 1))
            for r in range(4):
                down(DOWN0, r, r // 2 * 2, first=(r < 2))
            pe.wait_ge(ffn_low, led(ffn_low, FT))
            with pe.Fori(1, FT // 4) as i:
                for r in range(4):
                    down(i + DOWN0, r, i * 4 + r // 2 * 2)
            for r in range(2):
                down(DOWN0 + FT // 4, r, FT - 2, final=True)
            for j in range(KT // 2, KT):
                down_turn(j)


_INS = ["x", "norm_mix_w", "w_in", "conv_w", "a_log", "dt_bias", "gdn_norm_w", "fox_f_bias", "w_branch_a",
        "w_branch_b", "w_out", "norm_ffn_w", "w_gate", "w_up", "w_down", "norm_final_w"]


def kernel(**inputs):
    import numpy as _np
    import concourse.bacc as _bacc
    from concourse import mybir as _mybir
    from concourse.bass_utils import run_bass_kernel_spmd as _run

    nc = _bacc.Bacc("TRN2", target_bir_lowering=False, num_devices=1)
    arrays, args = {}, []
    for name in _INS:
        a = _np.ascontiguousarray(inputs[name])
        arrays[f"in_{name}"] = a
        args.append(nc.dram_tensor(f"in_{name}", a.shape, _mybir.dt.from_np(a.dtype), kind="ExternalInput").ap())
    shape = arrays["in_x"].shape
    args.append(nc.dram_tensor("out_0", shape, _mybir.dt.float32, kind="ExternalOutput").ap())
    hybrid_block(nc, *args)
    r = _run(nc, [arrays], core_ids=[0])
    return r.results[0]["out_0"]
```
